# Optimizing a Trainium2 kernel written in Bass

```python
import math
import jax, jax.numpy as jnp
from jax import lax
import numpy as np

D_MODEL = 1024
BATCH = 1
SEQ = 512
DEPTH = 4

N_MIXERS = 3
N_A = (DEPTH + 2) // 3
N_B = (DEPTH + 1) // 3
N_C = DEPTH // 3

RMS_EPS = 1e-6
LN_EPS = 1e-5
ROPE_THETA = 10000.0

D_FF = -(-8 * D_MODEL // (3 * 256)) * 256

GM_CHUNK = 128
GM_WIDTH = 2 * D_MODEL
GM_GROUPS = 8

NSA_HEADS = 16
NSA_KV_GROUPS = 4
NSA_HPG = NSA_HEADS // NSA_KV_GROUPS
NSA_HEAD_DIM = D_MODEL // NSA_HEADS
NSA_KV = NSA_KV_GROUPS * NSA_HEAD_DIM
CMP_LEN = 32
CMP_STRIDE = 16
CMP_HIDDEN = 4 * NSA_HEAD_DIM
SEL_LEN = 64
N_SELECT = 8
WIN = 512
NSA_Q_BLOCK = 64
NSA_IN = NSA_HEADS * NSA_HEAD_DIM + 6 * NSA_KV + 3 * NSA_HEADS

RET_HEADS = 4
RET_QK_DIM = D_MODEL // RET_HEADS
RET_V_DIM = 2 * RET_QK_DIM
RET_CHUNK = 128
RET_IN = 2 * RET_HEADS * RET_QK_DIM + 2 * RET_HEADS * RET_V_DIM

kernel_name = "hybrid_gmlp_nsa_retention_trunk"

def rms_norm(x, g):
    x32 = x.astype(jnp.float32)
    y = x32 * lax.rsqrt(jnp.mean(x32 * x32, axis=-1, keepdims=True) + RMS_EPS)
    return (y * g.astype(jnp.float32)).astype(x.dtype)

def layer_norm(x, g, b):
    x32 = x.astype(jnp.float32)
    mu = jnp.mean(x32, axis=-1, keepdims=True)
    var = jnp.mean(jnp.square(x32 - mu), axis=-1, keepdims=True)
    y = (x32 - mu) * lax.rsqrt(var + LN_EPS) * g.astype(jnp.float32) + b.astype(jnp.float32)
    return y.astype(x.dtype)

def apply_rope(x, pos):
    half = x.shape[-1] // 2
    inv = ROPE_THETA ** (-jnp.arange(half, dtype=jnp.float32) / half)
    ang = pos.astype(jnp.float32)[..., None] * inv
    cos = jnp.cos(ang)[:, :, None, :]
    sin = jnp.sin(ang)[:, :, None, :]
    x32 = x.astype(jnp.float32)
    x1, x2 = x32[..., :half], x32[..., half:]
    return jnp.concatenate([x1 * cos - x2 * sin, x2 * cos + x1 * sin], axis=-1).astype(x.dtype)

def masked_softmax(s, mask):
    s = s.astype(jnp.float32)
    m = jnp.max(jnp.where(mask, s, -jnp.inf), axis=-1, keepdims=True)
    m = jnp.where(jnp.isfinite(m), m, 0.0)
    e = jnp.where(mask, jnp.exp(s - m), 0.0)
    return e / jnp.maximum(jnp.sum(e, axis=-1, keepdims=True), 1e-30)

def swiglu_ffn(h, w_gate, w_up, w_down):
    return (jax.nn.silu(h @ w_gate) * (h @ w_up)) @ w_down

def gmlp_mixer(h, w_in, ln_g, ln_b, w_s, b_s, w_out):
    B, S, _ = h.shape
    uv = jax.nn.gelu(h @ w_in)
    u, v = jnp.split(uv, 2, axis=-1)
    v = layer_norm(v, ln_g, ln_b)
    v = v.reshape(B, S // GM_CHUNK, GM_CHUNK, GM_GROUPS, GM_WIDTH // GM_GROUPS)
    causal = jnp.tril(jnp.ones((GM_CHUNK, GM_CHUNK), dtype=bool))
    w_mix = jnp.where(causal, w_s, 0.0).astype(v.dtype)
    v = jnp.einsum('gts,bnsgc->bntgc', w_mix, v) + b_s.T[:, :, None].astype(v.dtype)
    return (u * v.reshape(B, S, GM_WIDTH)) @ w_out

def nsa_mixer(h, positions, w_in, cmp_pe, cmp_w1, cmp_w2, w_out):
    B, S, _ = h.shape
    H, G, HPG, dk = NSA_HEADS, NSA_KV_GROUPS, NSA_HPG, NSA_HEAD_DIM
    dt = h.dtype
    splits = np.cumsum([H * dk] + [NSA_KV] * 6).tolist()
    q, kc, vc, ks, vs, kw, vw, gates = jnp.split(h @ w_in, splits, axis=-1)
    q = apply_rope(q.reshape(B, S, H, dk), positions).reshape(B, S, G, HPG, dk)
    kc = kc.reshape(B, S, G, dk)
    vc = vc.reshape(B, S, G, dk)
    ks = apply_rope(ks.reshape(B, S, G, dk), positions)
    vs = vs.reshape(B, S, G, dk)
    kw = apply_rope(kw.reshape(B, S, G, dk), positions)
    vw = vw.reshape(B, S, G, dk)
    gates = jax.nn.sigmoid(gates.astype(jnp.float32)).reshape(B, S, G, HPG, 3)

    n_cmp = (S - CMP_LEN) // CMP_STRIDE + 1
    blk_idx = jnp.arange(n_cmp)[:, None] * CMP_STRIDE + jnp.arange(CMP_LEN)[None, :]
    cmp_end = blk_idx[:, -1]

    def compress(t, pe, w1, w2):
        blocks = t[:, blk_idx] + pe[:, None, :]
        blocks = jnp.moveaxis(blocks, 2, 3).reshape(B, n_cmp, G, CMP_LEN * dk)
        return jax.nn.gelu(blocks @ w1) @ w2

    k_cmp = apply_rope(compress(kc, cmp_pe[0], cmp_w1[0], cmp_w2[0]), positions[:, cmp_end])
    v_cmp = compress(vc, cmp_pe[1], cmp_w1[1], cmp_w2[1])

    n_sel = S // SEL_LEN
    k_top = min(N_SELECT, n_sel)
    ratio = SEL_LEN // CMP_STRIDE
    pad_c = n_sel * ratio - n_cmp
    ks_blk = ks.reshape(B, n_sel, SEL_LEN, G, dk).transpose(0, 3, 1, 2, 4)
    vs_blk = vs.reshape(B, n_sel, SEL_LEN, G, dk).transpose(0, 3, 1, 2, 4)
    sel_blocks = jnp.arange(n_sel)
    b_ix = jnp.arange(B)[:, None, None, None]
    g_ix = jnp.arange(G)[None, :, None, None]

    kw_pad = jnp.pad(kw, ((0, 0), (WIN, 0), (0, 0), (0, 0)))
    vw_pad = jnp.pad(vw, ((0, 0), (WIN, 0), (0, 0), (0, 0)))
    scale = dk ** -0.5
    T = NSA_Q_BLOCK

    def q_block(qi):
        t0 = qi * T
        tq = t0 + jnp.arange(T)
        qb = lax.dynamic_slice_in_dim(q, t0, T, axis=1)
        gb = lax.dynamic_slice_in_dim(gates, t0, T, axis=1)

        s_c = jnp.einsum('btghd,bngd->bghtn', qb, k_cmp) * scale
        p_c = masked_softmax(s_c, cmp_end[None, :] <= tq[:, None])
        o_c = jnp.einsum('bghtn,bngd->btghd', p_c.astype(dt), v_cmp)

        imp = jnp.pad(p_c.sum(axis=2), ((0, 0), (0, 0), (0, 0), (0, pad_c)))
        imp = imp.reshape(B, G, T, n_sel, ratio).sum(axis=-1)
        cur = tq // SEL_LEN
        forced = ((sel_blocks[None, :] == 0) | (sel_blocks[None, :] == cur[:, None])
                  | (sel_blocks[None, :] == cur[:, None] - 1))
        valid = sel_blocks[None, :] <= cur[:, None]
        imp = jnp.where(valid, jnp.where(forced, jnp.inf, imp), -jnp.inf)
        _, top = lax.top_k(imp, k_top)
        k_sel = ks_blk[b_ix, g_ix, top]
        v_sel = vs_blk[b_ix, g_ix, top]
        key_pos = top[..., None] * SEL_LEN + jnp.arange(SEL_LEN)
        m_s = (key_pos <= tq[None, None, :, None, None]).reshape(B, G, 1, T, k_top * SEL_LEN)
        s_s = jnp.einsum('btghd,bgtnkd->bghtnk', qb, k_sel) * scale
        p_s = masked_softmax(s_s.reshape(B, G, HPG, T, k_top * SEL_LEN), m_s)
        o_s = jnp.einsum('bghtnk,bgtnkd->btghd',
                         p_s.reshape(B, G, HPG, T, k_top, SEL_LEN).astype(dt), v_sel)

        kwb = lax.dynamic_slice_in_dim(kw_pad, t0, WIN + T, axis=1)
        vwb = lax.dynamic_slice_in_dim(vw_pad, t0, WIN + T, axis=1)
        kpos = t0 - WIN + jnp.arange(WIN + T)
        m_w = ((kpos[None, :] <= tq[:, None]) & (kpos[None, :] > tq[:, None] - WIN)
               & (kpos[None, :] >= 0))
        s_w = jnp.einsum('btghd,bsgd->bghts', qb, kwb) * scale
        p_w = masked_softmax(s_w, m_w)
        o_w = jnp.einsum('bghts,bsgd->btghd', p_w.astype(dt), vwb)

        o = gb[..., 0:1] * o_c + gb[..., 1:2] * o_s + gb[..., 2:3] * o_w
        return o.astype(dt).reshape(B, T, H * dk)

    out = lax.map(q_block, jnp.arange(S // T))
    out = jnp.moveaxis(out, 0, 1).reshape(B, S, H * dk)
    return out @ w_out

def retention_mixer(h, positions, w_in, gn_g, w_out):
    B, S, _ = h.shape
    H, dk, dv, C = RET_HEADS, RET_QK_DIM, RET_V_DIM, RET_CHUNK
    f32 = jnp.float32
    q, k, v, g = jnp.split(h @ w_in, [H * dk, 2 * H * dk, 2 * H * dk + H * dv], axis=-1)
    q = apply_rope(q.reshape(B, S, H, dk), positions).astype(f32)
    k = apply_rope(k.reshape(B, S, H, dk), positions).astype(f32) * (dk ** -0.5)
    v = v.reshape(B, S, H, dv).astype(f32)
    n_ch = S // C

    def chunks(t):
        return t.reshape(B, n_ch, C, H, t.shape[-1]).transpose(1, 0, 3, 2, 4)

    log_g = jnp.log1p(-(2.0 ** (-5.0 - jnp.arange(H, dtype=f32))))
    ix = jnp.arange(C, dtype=f32)
    rel = ix[:, None] - ix[None, :]
    decay = jnp.where(rel >= 0, jnp.exp(log_g[:, None, None] * jnp.maximum(rel, 0.0)), 0.0)
    xi = jnp.exp(log_g[:, None] * (ix + 1.0))
    zeta = jnp.exp(log_g[:, None] * (C - 1.0 - ix))
    g_chunk = jnp.exp(log_g * C)

    def step(state, qkv):
        qc, kc, vc = qkv
        inner = jnp.einsum('bhnm,bhme->bhne', jnp.einsum('bhnd,bhmd->bhnm', qc, kc) * decay, vc)
        cross = jnp.einsum('bhnd,bhde->bhne', qc, state) * xi[:, :, None]
        state = g_chunk[:, None, None] * state + jnp.einsum('bhmd,bhme->bhde', kc * zeta[:, :, None], vc)
        return state, inner + cross

    state0 = jnp.zeros((B, H, dk, dv), f32)
    _, o = lax.scan(step, state0, (chunks(q), chunks(k), chunks(v)))
    o = o.transpose(1, 0, 3, 2, 4).reshape(B, S, H, dv)
    mu = jnp.mean(o, axis=-1, keepdims=True)
    var = jnp.mean(jnp.square(o - mu), axis=-1, keepdims=True)
    o = ((o - mu) * lax.rsqrt(var + LN_EPS)).reshape(B, S, H * dv) * gn_g.astype(f32)
    y = (jax.nn.silu(g.astype(f32)) * o).astype(h.dtype)
    return y @ w_out

def setup_inputs(seed: int = 0) -> dict:
    key = jax.random.key(seed)
    ks = jax.random.split(key, 24)
    f32 = jnp.float32

    def dense(k, shape, fan_in):
        return jax.random.normal(k, shape, f32) * (fan_in ** -0.5)

    def gain(k, shape):
        return 1.0 + 0.05 * jax.random.normal(k, shape, f32)

    x = jax.random.normal(ks[0], (BATCH, SEQ, D_MODEL), f32)
    offs = jax.random.randint(ks[1], (BATCH, 1), 0, 4096, dtype=jnp.int32)
    positions = (offs + jnp.arange(SEQ, dtype=jnp.int32)[None, :]).astype(jnp.int32)
    return {
        "x": x,
        "positions": positions,
        "norm_g": gain(ks[2], (DEPTH, 4, D_MODEL)),
        "ffn_w_gate": dense(ks[3], (DEPTH, D_MODEL, D_FF), D_MODEL),
        "ffn_w_up": dense(ks[4], (DEPTH, D_MODEL, D_FF), D_MODEL),
        "ffn_w_down": dense(ks[5], (DEPTH, D_FF, D_MODEL), D_FF),
        "gm_w_in": dense(ks[6], (N_A, D_MODEL, 2 * GM_WIDTH), D_MODEL),
        "gm_ln_g": gain(ks[7], (N_A, GM_WIDTH)),
        "gm_ln_b": 0.02 * jax.random.normal(ks[8], (N_A, GM_WIDTH), f32),
        "gm_w_s": dense(ks[9], (N_A, GM_GROUPS, GM_CHUNK, GM_CHUNK), GM_CHUNK),
        "gm_b_s": 1.0 + 0.1 * jax.random.normal(ks[10], (N_A, GM_GROUPS, GM_CHUNK), f32),
        "gm_w_out": dense(ks[11], (N_A, GM_WIDTH, D_MODEL), GM_WIDTH),
        "nsa_w_in": dense(ks[12], (N_B, D_MODEL, NSA_IN), D_MODEL),
        "nsa_cmp_pe": 0.1 * jax.random.normal(ks[13], (N_B, 2, CMP_LEN, NSA_HEAD_DIM), f32),
        "nsa_cmp_w1": dense(ks[14], (N_B, 2, CMP_LEN * NSA_HEAD_DIM, CMP_HIDDEN), CMP_LEN * NSA_HEAD_DIM),
        "nsa_cmp_w2": dense(ks[15], (N_B, 2, CMP_HIDDEN, NSA_HEAD_DIM), CMP_HIDDEN),
        "nsa_w_out": dense(ks[16], (N_B, NSA_HEADS * NSA_HEAD_DIM, D_MODEL), NSA_HEADS * NSA_HEAD_DIM),
        "ret_w_in": dense(ks[17], (N_C, D_MODEL, RET_IN), D_MODEL),
        "ret_gn_g": gain(ks[18], (N_C, RET_HEADS * RET_V_DIM)),
        "ret_w_out": dense(ks[19], (N_C, RET_HEADS * RET_V_DIM, D_MODEL), RET_HEADS * RET_V_DIM),
    }

def reference(x, positions, norm_g, ffn_w_gate, ffn_w_up, ffn_w_down,
              gm_w_in, gm_ln_g, gm_ln_b, gm_w_s, gm_b_s, gm_w_out,
              nsa_w_in, nsa_cmp_pe, nsa_cmp_w1, nsa_cmp_w2, nsa_w_out,
              ret_w_in, ret_gn_g, ret_w_out):
    h = x
    for i in range(DEPTH):
        kind, j = i % N_MIXERS, i // N_MIXERS
        a = rms_norm(h, norm_g[i, 0])
        if kind == 0:
            m = gmlp_mixer(a, gm_w_in[j], gm_ln_g[j], gm_ln_b[j], gm_w_s[j], gm_b_s[j], gm_w_out[j])
        elif kind == 1:
            m = nsa_mixer(a, positions, nsa_w_in[j], nsa_cmp_pe[j], nsa_cmp_w1[j],
                          nsa_cmp_w2[j], nsa_w_out[j])
        else:
            m = retention_mixer(a, positions, ret_w_in[j], ret_gn_g[j], ret_w_out[j])
        h = h + rms_norm(m, norm_g[i, 1])
        f = swiglu_ffn(rms_norm(h, norm_g[i, 2]), ffn_w_gate[i], ffn_w_up[i], ffn_w_down[i])
        h = h + rms_norm(f, norm_g[i, 3])
    return h


_drawn_inputs = setup_inputs


def setup_inputs(seed=0):
    import zlib

    import numpy as np

    out = dict(_drawn_inputs(seed))
    spreads = {}
    factors = {'gm_ln_b': 4.012}
    for name, (base, spread) in spreads.items():
        noise = np.random.default_rng([zlib.crc32(name.encode()), seed]).standard_normal(out[name].shape)
        drawn = base * np.exp(spread * noise) if base else spread * noise
        out[name] = __import__('jax').numpy.asarray(drawn.astype(out[name].dtype))
    for name, factor in factors.items():
        out[name] = (out[name] * factor).astype(out[name].dtype)
    return out
```

```python
from contextlib import ExitStack

import numpy as np

import concourse.bass as bass
from concourse import mybir

P = 128
SEQ = 512
D_MODEL = 1024
DT = D_MODEL // P
CH = SEQ // P
D_FF = 2816
FT = D_FF // P
KMAX = 8
SLOTS = 4
AHEAD = 3
BANKS = 4
RMS_EPS = 1e-6
ROPE_THETA = 10000.0
LN_EPS = 1e-5

GM_WIDTH = 2048
GM_TILES = GM_WIDTH // P
GM_GROUPS = 8

H_NSA = 16
G_NSA = 4
HD = 64
N_CMP = 31
CMP_LEN = 32
CMP_STRIDE = 16
CMP_HIDDEN = 256
NSA_SCALE = HD ** -0.5
MASKED = -1e30

RH = 4
R_QK = 256
R_V = 512

f32 = mybir.dt.float32
f32r = mybir.dt.float32r
i32 = mybir.dt.int32
ACT = mybir.ActivationFunctionType
ALU = mybir.AluOpType
AX = mybir.AxisListType

ONE = [8]
TWO = [8, 8]
THREE = [8, 8, 6]


PI = float(np.nextafter(np.float32(np.pi), np.float32(0)))
ROUNDER = 1.5 * 2.0 ** 23


def _two_pi():
    a = 6.28125
    b = float(np.round((2 * np.pi - a) * 2 ** 20) / 2 ** 20)
    return a, b, float(np.float32(2 * np.pi - a - b))


TWO_PI = _two_pi()


NSA_UNITS = ([(m * P, "q") for m in range(8)] + [(1024 + m * P, "kc") for m in range(2)] + [(1280 + m * P, "vc") for m in range(2)]
             + [(1536 + m * P, "ks") for m in range(2)] + [(1792 + m * P, "vs") for m in range(2)]
             + [(2048 + m * P, "kw") for m in range(2)] + [(2304 + m * P, "vw") for m in range(2)] + [(2480, "gate")])
NSA_GATE0 = 80
PAIRS = [(c, br, hp) for c in range(CH) for br in range(2) for hp in range(H_NSA // 2)]


def nth(u, kinds):
    return sum(kind in kinds for _, kind in NSA_UNITS[:u])


ROPED = ("q", "ks", "kw")
VALUES = ("vs", "vw", "gate")


def loop(eng, iters, step, peel_first=0, peel_last=0):
    for i in range(peel_first):
        step(i)
    middle = iters - peel_first - peel_last
    if middle > 0:
        with eng.Fori(0, middle) as r:
            step(r + peel_first if peel_first else r)
    for i in range(iters - peel_last, iters):
        step(i)


def wait(eng, sem, value):
    if not isinstance(value, int) or value > 0:
        eng.wait_ge(sem, value)


def plan(layers):
    n = o = b = q = trig = sine = tab = 0
    out = []
    z = {0: 0, 1: 0, 2: 0}
    for layer in layers:
        kind = layer % 3
        L = {"layer": layer, "kind": kind, "z": z[kind]}
        z[kind] += 1
        L["b_in"] = b
        L["trig"], L["sine"], L["tab"] = trig, sine, tab
        trig, sine, tab = trig + {0: 0, 1: 2, 2: 4}[kind], sine + {0: 0, 1: 2, 2: 2}[kind], tab + {0: 0, 1: 32, 2: 48}[kind]
        L["n_in"], L["o_in"] = n, o
        n, o = n + {0: 32, 1: 21, 2: 48}[kind], o + {0: 32, 1: 21, 2: 80}[kind]
        L["n_out"], L["o_out"] = n, o
        n, o = n + {0: 16, 1: 8, 2: 16}[kind], o + 8
        b += 1
        L["b_mid"] = b
        L["n_up"], L["o_up"], L["q_up"] = n, o, q
        n, o, q = n + 2 * FT, o + 2 * FT, q + FT
        L["n_down"], L["o_down"] = n, o
        n, o = n + 24, o + 8
        b += 1
        L["b_end"] = b
        out.append(L)
    return out, n, o, b


def build(nc, x, positions, norm_g, ffn_w_gate, ffn_w_up, ffn_w_down,
          gm_w_in, gm_ln_g, gm_ln_b, gm_w_s, gm_b_s, gm_w_out,
          nsa_w_in, nsa_cmp_pe, nsa_cmp_w1, nsa_cmp_w2, nsa_w_out,
          ret_w_in, ret_gn_g, ret_w_out, c_identity, c_freq, c_decay, c_perm, c_causal, c_cmp_bias, c_cmp_keep, out, layers=(0, 1, 2, 3)):
    PL, N_UNITS, N_OUTS, N_BOUND = plan(layers)
    ctx = ExitStack()
    with ctx:
        at = [(nc.sbuf_base + 63) // 64 * 64]

        def place(name, shape, dt=f32, offset=None):
            size = int(np.prod(shape[1:])) * 4
            if offset is None:
                offset = at[0]
                at[0] += size
            return nc.alloc_sbuf_tensor_at(name, shape, dt, offset=offset)

        h = place("h", [P, DT, SEQ])
        a_hi = place("a_hi", [P, DT, SEQ], f32r)
        off_lo = at[0]
        a_lo = place("a_lo", [P, DT, SEQ], f32r)
        F = place("F", [P, DT, SEQ], f32, off_lo)
        w_raw = place("w_raw", [P, SLOTS, KMAX, P])
        w_hi = place("w_hi", [P, SLOTS, KMAX, P], f32r)
        w_lo = place("w_lo", [P, SLOTS, KMAX, P], f32r)
        B = at[0]
        at[0] += 2 * FT * SEQ * 4
        work = place("work", [P, 6, SEQ])
        sq = place("sq", [P, 2, SEQ])
        SS = place("SS", [P, SEQ])
        R = place("R", [P, SEQ])
        ones = place("ones", [P, P])
        ident = place("ident", [P, P])
        gain = place("gain", [P, 16, DT])
        lnp = place("lnp", [P, 112])
        r4 = place("r4", [P, 8])
        rows = place("rows", [P, P])
        assert at[0] <= nc.sbuf_usable_end, (at[0], nc.sbuf_usable_end)
        KB = 1024
        hid_hi = place("hid_hi", [P, FT, SEQ], f32r, B)
        hid_lo = place("hid_lo", [P, FT, SEQ], f32r, B + 44 * KB)
        x_tok = place("x_tok", [P, CH, D_MODEL], f32, B)
        y_tok = place("y_tok", [P, CH, D_MODEL], f32, B)
        gv = place("gv", [P, GM_TILES, SEQ], f32, B)
        g_hi = place("g_hi", [P, GM_TILES, SEQ], f32r, B)
        gu = place("gu", [P, GM_TILES, SEQ], f32, B + 32 * KB)
        g_lo = place("g_lo", [P, GM_TILES, SEQ], f32r, B + 32 * KB)
        ws_raw = place("ws_raw", [P, GM_GROUPS, P], f32, B + 64 * KB)
        ws_hi = place("ws_hi", [P, GM_GROUPS, P], f32r, B + 68 * KB)
        ws_lo = place("ws_lo", [P, GM_GROUPS, P], f32r, B + 72 * KB)
        bs = place("bs", [P, GM_GROUPS, P], f32, B + 76 * KB)
        vt_hi = place("vt_hi", [P, 2, CH, P], f32r, B + 80 * KB)
        vt_lo = place("vt_lo", [P, 2, CH, P], f32r, B + 84 * KB)

        rq = place("rq", [P, 2, SEQ], f32, B)
        rk = place("rk", [P, 2, SEQ], f32, B + 4 * KB)
        rv = place("rv", [P, CH, R_V], f32, B + 8 * KB)
        rg = place("rg", [P, 4, SEQ], f32, B + 16 * KB)
        ro = place("ro", [P, 4, SEQ], f32, B + 24 * KB)
        y_hi_tail = place("y_hi_tail", [P, 8, SEQ], f32r, B)
        y_hi = [a_hi[:, t, :] for t in range(8)] + [y_hi_tail[:, t, :] for t in range(8)]
        ry = place("ry", [P, 16, SEQ], f32, B + 32 * KB)
        y_lo = place("y_lo", [P, 16, SEQ], f32r, B + 32 * KB)
        decay = place("decay", [P, RH, SEQ], f32, B + 64 * KB)
        r_cos = place("r_cos", [P, SEQ], f32, B + 72 * KB)
        r_sin = place("r_sin", [P, SEQ], f32, B + 74 * KB)
        rp = [place(f"rp{m}", [P, SEQ - m * P], f32, B + 76 * KB + sum(SEQ - k * P for k in range(m)) * 4) for m in range(CH)]
        r_mu = place("r_mu", [P, SEQ], f32, B + 81 * KB)
        r_sd = place("r_sd", [P, SEQ], f32, B + 83 * KB)
        pos_i = place("pos_i", [P, SEQ], i32, B + 85 * KB)
        freq = place("freq", [P, 2], f32, B + 87 * KB)

        nq = place("nq", [P, 8, SEQ], f32, B)
        kd = place("kd", [P, 2, G_NSA, SEQ], f32, B + 16 * KB)
        o_hi = place("o_hi", [P, DT, SEQ], f32r, B)
        o_lo = place("o_lo", [P, DT, SEQ], f32r, B + 16 * KB)
        vt = place("vt", [P, 2, CH, 2 * P], f32, B + 32 * KB)
        kc2 = place("kc2", [P, 2, G_NSA, SEQ], f32, B + 40 * KB)
        gt = place("gt", [P, CH, P], f32, B + 56 * KB)
        n_cos = place("n_cos", [P, SEQ], f32, B + 58 * KB)
        n_sin = place("n_sin", [P, SEQ], f32, B + 60 * KB)
        cmp_bias = place("cmp_bias", [P, CH, 32], f32, B + 62 * KB)
        cmp_keep = place("cmp_keep", [P, CH, 32], f32, B + 62 * KB + 512)
        kcr = place("kcr", [P, G_NSA, 32], f32, B + 63 * KB)
        causal_r = place("causal_r", [P, P], f32r, B + 63 * KB + 512)
        ident_r = place("ident_r", [P, P], f32r, B + 64 * KB)
        causal = place("causal", [P, P], f32, B + 64 * KB + 512)
        vblk = place("vblk", [P, G_NSA, 2 * P], f32, B + 65 * KB)
        w2 = place("w2", [P, 2, 2, P], f32, B + 69 * KB)
        perm = place("perm", [P, P], f32, B + 71 * KB)
        h1k = place("h1k", [P, 2, G_NSA, 32], f32, B + 72 * KB)
        h1v = place("h1v", [P, 2, G_NSA, P], f32, B + 75 * KB)
        stg = place("stg", [P, 2, G_NSA, 32], f32, B + 74 * KB)
        pt = place("pt", [P, 4, SEQ], f32, off_lo)
        ex = place("ex", [P, 4, SEQ], f32, B + 79 * KB)
        SM = B + 87 * KB + 64
        nm = place("nm", [P, 4, 2], f32, SM)
        rs = place("rs", [P, 2, H_NSA], f32, SM + 32)
        scl = place("scl", [P, 2, H_NSA], f32, SM + 160)
        cmx = place("cmx", [P, CH, H_NSA], f32, SM + 288)
        csm = place("csm", [P, CH, H_NSA], f32, SM + 544)
        off_a = off_lo - 16 * KB
        w1 = place("w1", [P, 2, 16, CMP_HIDDEN], f32, off_a)
        otok = place("otok", [P, CH, D_MODEL], f32, off_a)

        def psum(name, n):
            return ctx.enter_context(nc.psum_tensor(name, [P, n, SEQ], f32))

        acc = psum("acc", BANKS)
        tr = psum("tr", 2)
        st = psum("st", 2)

        def sem(name):
            return ctx.enter_context(nc.semaphore(name))

        loaded = [sem(f"loaded{s}") for s in range(SLOTS)]
        names = """id_in params cols_done gain_ready ones_ready x_in x_tr h_init
            hi_done lo_done unit_done acc_free f_sq ss_sum stat_f stat_h stat_rd root_done r_ready
            r4_ready r_spread f_scaled h_new a_hi_done h_sq a_lo_done
            silu_done hid_mul hid_hi_done hid_lo_done
            gelu_done vsum mean_mm mu_ready v_cen c_sq csum var_mm var_rd var_root rstd_ready
            ws_in bs_in ws_masked ws_tr ws_hi_done ws_lo_done
            vn_done vb_done vt_done vt_hi_done vt_lo_done mix_done xb_done pm_done g_hi_done g_lo_done
            tab_in trig_step trig_ready sin_done rope_out rv_tr rv_done rs_done ro_done
            o_sum r_mean_mm r_mu_ready ro_cen ro_sq ro_csum r_var_mm r_var_rd r_root r_sd_ready ry_done rg_done y_hi_done y_lo_done
            n_tab_in w1k_in w1v_in n_zero rot_done rope_t n_rope kd_dup kc_done nv_tr nv_done sig_done gt_done mask_r
            stg_ready cmp_mm h1_done kcmp_mm kcmp_x kcmp_rot kcmp_done vcmp_mm vblk_done
            sc_even sc_mm sm_done pexp pc_done pc_tr pc_t pvc_mm ocmp_done dve_step
            s_mm max_done exp_done t_mm pt_done pv_mm rs_inv o_rd o_add ot_tr o_hi_done o_lo_done
            y_tr y_sb stored""".split()
        s = {n: sem(n) for n in names}
        (id_in, params, cols_done, gain_ready, ones_ready, x_in, x_tr, h_init,
         hi_done, lo_done, unit_done, acc_free, f_sq, ss_sum, stat_f, stat_h, stat_rd, root_done, r_ready,
         r4_ready, r_spread, f_scaled, h_new, a_hi_done, h_sq, a_lo_done,
         silu_done, hid_mul, hid_hi_done, hid_lo_done,
         gelu_done, vsum, mean_mm, mu_ready, v_cen, c_sq, csum, var_mm, var_rd, var_root, rstd_ready,
         ws_in, bs_in, ws_masked, ws_tr, ws_hi_done, ws_lo_done,
         vn_done, vb_done, vt_done, vt_hi_done, vt_lo_done, mix_done, xb_done, pm_done, g_hi_done, g_lo_done,
         tab_in, trig_step, trig_ready, sin_done, rope_out, rv_tr, rv_done, rs_done, ro_done,
         o_sum, r_mean_mm, r_mu_ready, ro_cen, ro_sq, ro_csum, r_var_mm, r_var_rd, r_root, r_sd_ready, ry_done, rg_done, y_hi_done, y_lo_done,
         n_tab_in, w1k_in, w1v_in, n_zero, rot_done, rope_t, n_rope, kd_dup, kc_done, nv_tr, nv_done, sig_done, gt_done, mask_r,
         stg_ready, cmp_mm, h1_done, kcmp_mm, kcmp_x, kcmp_rot, kcmp_done, vcmp_mm, vblk_done,
         sc_even, sc_mm, sm_done, pexp, pc_done, pc_tr, pc_t, pvc_mm, ocmp_done, dve_step,
         s_mm, max_done, exp_done, t_mm, pt_done, pv_mm, rs_inv, o_rd, o_add, ot_tr, o_hi_done, o_lo_done,
         y_tr, y_sb, stored) = [s[n] for n in names]

        def tile(ap, k):
            return ap[k] if isinstance(ap, list) else ap[:, k, :]

        def mix_bank(L, m):
            return (L["o_out"] + 2 + m % 2) % BANKS

        def side_of(hd):
            return slice(HD * (hd % 2), HD * (hd % 2) + HD)

        def pair_bank(p):
            return acc[:, 0:2, :] if p % 2 == 0 else st[:, :, :]

        block = ctx.enter_context(nc.Block())

        @block.sync
        def _(sp):
            def load(n, slot, src, kt):
                wait(sp, lo_done, n - SLOTS + 1)
                sp.dma_start(w_raw[:, slot, 0:kt, :], src.rearrange("(k p) m -> p k m", p=P)).then_inc(loaded[slot], 16)

            def stream(n0, iters, U, src, kts, peel_first=0):
                def step(i):
                    for j in range(U):
                        load(i * U + (n0 + j), (n0 + j) % SLOTS, src(i, j), kts[j % len(kts)])
                loop(sp, iters, step, peel_first)

            def cols(w, r0, r1, c):
                return w[r0:r1, c:c + P] if isinstance(c, int) else w[r0:r1, bass.ds(c, P)]

            sp.dma_start(rows[:, :], norm_g.rearrange("l n (t p) -> (l n t) p", p=P)).then_inc(params, 16)
            sp.wait_ge(cols_done, 1)
            sp.dma_start(rows[0:32, :], gm_ln_g.rearrange("z (t p) -> (z t) p", p=P)).then_inc(params, 16)
            sp.dma_start(rows[32:64, :], gm_ln_b.rearrange("z (t p) -> (z t) p", p=P)).then_inc(params, 16)
            sp.dma_start(rows[64:80, :], ret_gn_g.rearrange("z (t p) -> (z t) p", p=P)).then_inc(params, 16)
            sp.dma_start(rows[80:112, :], nsa_cmp_pe[0].rearrange("b (j l) d -> (b j) (l d)", l=2)).then_inc(params, 16)
            for L in PL:
                l, z = L["layer"], L["z"]
                first = 1 if L["n_in"] == 0 else 0
                if L["kind"] == 0:
                    def gm_in(half):
                        return lambda i, j: cols(gm_w_in[z], 0, D_MODEL, i * (4 * P) + (half + j * P))
                    stream(L["n_in"], 4, 4, gm_in(GM_WIDTH), ONE, first)
                    sp.wait_ge(a_lo_done, 8 * (L["b_in"] + 1))
                    sp.dma_start(ws_raw[:, :, :], gm_w_s[z].rearrange("g t s -> t g s")).then_inc(ws_in, 16)
                    sp.dma_start(bs[:, :, :], gm_b_s[z].partition_broadcast(P)).then_inc(bs_in, 16)
                    stream(L["n_in"] + 16, 4, 4, gm_in(0), ONE)
                    stream(L["n_out"], 2, 8,
                           lambda i, j: cols(gm_w_out[z], (j % 2) * 1024, (j % 2) * 1024 + 1024, i * (4 * P) + (j // 2) * P), TWO)
                if L["kind"] == 1:
                    for u, (c0, _) in enumerate(NSA_UNITS):
                        load(L["n_in"] + u, (L["n_in"] + u) % SLOTS, nsa_w_in[z, :, c0:c0 + P], DT)
                    stream(L["n_out"], 2, 4, lambda i, j: cols(nsa_w_out[z], 0, D_MODEL, i * (4 * P) + j * P), ONE)
                if L["kind"] == 2:
                    def ret_in(i, j):
                        base, width = [(0, R_QK), (1024, R_QK), (2048, R_V), (4096, R_V)][[0, 0, 1, 1, 2, 2, 2, 2, 3, 3, 3, 3][j]]
                        return cols(ret_w_in[z], 0, D_MODEL, i * width + (base + (j % 2 if j < 4 else j % 4) * P))
                    stream(L["n_in"], RH, 12, ret_in, ONE, first)
                    stream(L["n_out"], 2, 8,
                           lambda i, j: cols(ret_w_out[z], (j % 2) * 1024, (j % 2) * 1024 + 1024, i * (4 * P) + (j // 2) * P), TWO)
                stream(L["n_up"], 11, 4,
                       lambda i, j: cols((ffn_w_gate if j % 2 == 0 else ffn_w_up)[l], 0, D_MODEL, i * (2 * P) + (j // 2) * P), ONE)
                stream(L["n_down"], 2, 12,
                       lambda i, j: cols(ffn_w_down[l], (j % 3) * 1024, min((j % 3) * 1024 + 1024, D_FF), i * (4 * P) + (j // 3) * P), THREE)
            for c in range(CH):
                sp.wait_ge(y_sb, 2 * (c + 1))
                sp.dma_start(out[0, c * P:(c + 1) * P, :], y_tok[:, c, :]).then_inc(stored, 16)
            sp.wait_ge(stored, 16 * CH)

        @block.tensor
        def _(pe):
            def product(o_bank, lhs_hi, lhs_lo, rhs_hi, rhs_lo, start, stop):
                pe.matmul(o_bank, lhs_hi, rhs_hi, start=start, stop=False)
                pe.matmul(o_bank, lhs_hi, rhs_lo, start=False, stop=False)
                return pe.matmul(o_bank, lhs_lo, rhs_hi, start=False, stop=stop)

            def entry_unit(b, n, slot, bank):
                wait(pe, lo_done, n + 1)
                wait(pe, acc_free, acc_before(n))
                wait(pe, stat_rd, 2 * b)
                for k in range(DT):
                    pe.wait_ge(a_lo_done, DT * b + k + 1)
                    last = product(acc[:, bank, :], w_hi[:, slot, k, :], w_lo[:, slot, k, :], a_hi[:, k, :], a_lo[:, k, :],
                                   k == 0, k == DT - 1)
                    if k == DT - 1:
                        last.then_inc(unit_done, 1)
                    pe.wait_ge(h_sq, DT * b + k + 1)
                    pe.matmul(st[:, 0, :], ones[:, :], sq[:, k % 2, :], start=k == 0, stop=k == DT - 1).then_inc(stat_h, 1)

            def acc_before(n):
                return {**{x["n_in"]: x["o_in"] for x in PL}, **{x["n_up"]: x["o_up"] for x in PL}}[n]

            def piece(n0, o0, G, j, k, rhs_hi, rhs_lo):
                slot, bank, kk = (n0 + j) % SLOTS, (o0 + j // G) % BANKS, (j % G) * KMAX + k
                if k == 0:
                    pe.wait_ge(lo_done, n0 + j + 1)
                    if j % G == 0:
                        wait(pe, acc_free, o0 + j // G - BANKS + 1)
                last = product(acc[:, bank, :], w_hi[:, slot, k, :], w_lo[:, slot, k, :], rhs_hi[:, kk, :], rhs_lo[:, kk, :],
                               kk == 0, kk == G * KMAX - 1)
                if k == KMAX - 1:
                    last.then_inc(unit_done, 1)

            def dense(n0, o0, iters, U, kts, rhs_hi, rhs_lo, peel_first=0, after=None, entry=None, begun=0, operand=None):
                G = len(kts)
                if entry is not None or begun or operand:
                    peel_first = 1
                oU = U // G

                def step(i):
                    for j in range(U):
                        slot, bank, t = (n0 + j) % SLOTS, (o0 + j // G) % BANKS, j % G
                        if entry is not None and isinstance(i, int) and j == 0:
                            entry_unit(entry, n0, slot, bank)
                            continue
                        if isinstance(i, int) and i * U + j < begun:
                            continue
                        pe.wait_ge(lo_done, i * U + (n0 + j + 1))
                        if t == 0:
                            wait(pe, acc_free, i * oU + (o0 + j // G - BANKS + 1))
                        for k in range(kts[t]):
                            kk = sum(kts[:t]) + k
                            if operand and isinstance(i, int) and i == 0 and j < G:
                                pe.wait_ge(operand[0], operand[1] + kk + 1)
                            last = product(acc[:, bank, :], w_hi[:, slot, k, :], w_lo[:, slot, k, :],
                                           tile(rhs_hi, kk), rhs_lo[:, kk, :],
                                           t == 0 and k == 0, t == G - 1 and k == kts[t] - 1)
                        last.then_inc(unit_done, 1)
                        if after:
                            after(i, j)
                loop(pe, iters, step, peel_first)

            def boundary(b):
                pe.wait_ge(ss_sum, 9 * b)
                pe.wait_ge(stat_rd, 2 * b - 1)
                for c in range(CH):
                    last = pe.matmul(st[:, 0, c:c + 1], SS[:, c * P:(c + 1) * P], ones[:, 0:1], start=True, stop=True)
                last.then_inc(stat_f, 1)
                pe.wait_ge(r4_ready, b)
                for c in range(CH):
                    last = pe.transpose(st[:, 1, c * P:(c + 1) * P], r4[:, c:c + 1].broadcast_to([P, P]), ident[:, :])
                last.then_inc(r_spread, 1)

            def gmlp_mix(L):
                z = L["z"]
                pe.wait_ge(csum, 17 * (z + 1))
                pe.wait_ge(mu_ready, z + 1)
                pe.matmul(st[:, 0, :], ones[:, :], SS[:, :], start=True, stop=True).then_inc(var_mm, 1)
                pe.wait_ge(ws_masked, z + 1)
                for g in range(GM_GROUPS):
                    last = pe.transpose(tr[:, g // 4, (g % 4) * P:(g % 4 + 1) * P], ws_raw[:, g, :], ident[:, :])
                last.then_inc(ws_tr, 1)
                pe.wait_ge(ws_lo_done, z + 1)
                pe.wait_ge(acc_free, L["o_out"])
                M = GM_TILES
                for k in range(M + 4):
                    if k < M:
                        pe.wait_ge(vb_done, M * z + k + 1)
                        wait(pe, vt_lo_done, M * z + k - 1)
                        for c in range(CH):
                            last = pe.transpose(tr[:, k % 2, c * P:(c + 1) * P], work[:, k % 2, c * P:(c + 1) * P], ident[:, :])
                        last.then_inc(vt_done, 1)
                    m = k - 1
                    if 0 <= m < M:
                        pe.wait_ge(vt_lo_done, M * z + m + 1)
                        wait(pe, xb_done, M * z + m - 1)
                        for c in range(CH):
                            last = product(acc[:, mix_bank(L, m), c * P:(c + 1) * P], vt_hi[:, m % 2, c, :], vt_lo[:, m % 2, c, :],
                                           ws_hi[:, m // 2, :], ws_lo[:, m // 2, :], True, True)
                        last.then_inc(mix_done, 1)
                    m = k - 4
                    if m >= 0:
                        pe.wait_ge(g_lo_done, M * z + m + 1)
                        piece(L["n_out"], L["o_out"], 2, m // KMAX, m % KMAX, g_hi, g_lo)
                        if m >= KMAX:
                            piece(L["n_out"], L["o_out"], 2, 2, m - KMAX, g_hi, g_lo)
                pe.wait_ge(xb_done, M * (z + 1))

            def attention(L):
                n0, o0 = L["n_in"], L["o_in"]

                def bank_read(u):
                    while u >= 0:
                        kind = NSA_UNITS[u][1]
                        if kind in ROPED:
                            return pe.wait_ge(rope_t, nth(u, ROPED) + 1)
                        if kind in VALUES:
                            return pe.wait_ge(nv_done, nth(u, VALUES) + 1)
                        u -= 2

                for u in range(len(NSA_UNITS) + 1):
                    if u < len(NSA_UNITS):
                        slot, bank = (n0 + u) % SLOTS, (o0 + u) % BANKS
                        if u == 0:
                            entry_unit(L["b_in"], n0, slot, bank)
                        else:
                            pe.wait_ge(lo_done, n0 + u + 1)
                            wait(pe, acc_free, o0 + u - BANKS + 1)
                            for k in range(DT):
                                last = product(acc[:, bank, :], w_hi[:, slot, k, :], w_lo[:, slot, k, :],
                                               a_hi[:, k, :], a_lo[:, k, :], k == 0, k == DT - 1)
                            last.then_inc(unit_done, 1)
                    v = u - 1
                    if v < 0:
                        pe.wait_ge(n_tab_in, 16 * 7)
                        continue
                    kind = NSA_UNITS[v][1]
                    if kind in ROPED:
                        pe.wait_ge(acc_free, o0 + v + 1)
                        bank_read(v - 2)
                        pe.matmul(tr[:, v % 2, :], perm[:, :], work[:, v % 2, :], start=True, stop=True).then_inc(rot_done, 1)
                    elif kind in VALUES:
                        pe.wait_ge(acc_free, o0 + v + 1)
                        if kind == "gate":
                            pe.wait_ge(sig_done, 1)
                        bank_read(v - 2)
                        for c in range(CH):
                            last = pe.transpose(tr[:, v % 2, c * P:(c + 1) * P], work[:, v % 2, c * P:(c + 1) * P], ident[:, :])
                        last.then_inc(nv_tr, 1)
                pe.wait_ge(acc_free, o0 + len(NSA_UNITS))
                for br in range(2):
                    pe.wait_ge(w1v_in if br else w1k_in, 16)
                    for j in range(16):
                        pe.wait_ge(stg_ready, 16 * br + j + 1)
                        for hh in range(2):
                            last = pe.matmul(acc[:, 2 * br + hh, 0:G_NSA * 32].rearrange("p (g n) -> p g n", g=G_NSA)[:, :, 0:N_CMP],
                                             w1[:, br, j, hh * P:(hh + 1) * P], stg[:, j % 2, :, 0:N_CMP], start=j == 0, stop=j == 15)
                        last.then_inc(cmp_mm, 1)
                pe.wait_ge(h1_done, 2)
                pe.wait_ge(rope_t, 12)
                pe.wait_ge(nv_done, 5)
                for hh in range(2):
                    last = pe.matmul(tr[:, 0, 0:G_NSA * N_CMP].rearrange("p (g n) -> p g n", g=G_NSA), w2[:, 0, hh, :], h1k[:, hh, :, 0:N_CMP], start=hh == 0, stop=hh == 1)
                last.then_inc(kcmp_mm, 1)
                pe.wait_ge(h1_done, 4)
                pe.wait_ge(n_zero, 4)
                for g in range(G_NSA):
                    for hh in range(2):
                        last = pe.matmul(st[:, 0, g * HD:(g + 1) * HD],
                                         h1v[:, hh, g, :], w2[:, 1, hh, 0:HD],
                                         start=hh == 0, stop=hh == 1)
                last.then_inc(vcmp_mm, 1)
                pe.wait_ge(kcmp_x, 1)
                pe.matmul(tr[:, 1, 0:G_NSA * N_CMP], perm[:, :], work[:, 0, 0:G_NSA * N_CMP], start=True, stop=True).then_inc(kcmp_rot, 1)
                pe.wait_ge(kcmp_done, 1)
                pe.wait_ge(n_rope, 12)
                pe.wait_ge(kd_dup, 4)
                for c in range(CH + 1):
                    if c < CH:
                        wait(pe, sm_done, c - 1)
                        for hd in [*range(0, H_NSA, 2), *range(1, H_NSA, 2)]:
                            if hd == 1:
                                last.then_inc(sc_even, 1)
                                pe.wait_ge(sc_even, c + 1)
                            last = pe.matmul(acc[:, c % 2, 32 * hd:32 * hd + N_CMP], nq[side_of(hd), hd // 2, c * P:(c + 1) * P],
                                             kcr[side_of(hd), hd // 4, 0:N_CMP], start=True, stop=True)
                        last.then_inc(sc_mm, 1)
                    v = c - 1
                    if v >= 0:
                        pe.wait_ge(pc_done, v + 1)
                        wait(pe, pc_t, v - 1)
                        for g in range(G_NSA):
                            last = pe.transpose(tr[:, v % 2, g * P:(g + 1) * P], ex[:, v % 2, g * P:(g + 1) * P], ident[:, :])
                        last.then_inc(pc_tr, 1)
                        pe.wait_ge(pc_t, v + 1)
                        pe.wait_ge(vblk_done, 4)
                        wait(pe, ocmp_done, v)
                        for g in range(G_NSA):
                            last = pe.matmul(acc[:, 2 + g // 2, (g % 2) * 2 * P:(g % 2 + 1) * 2 * P], pt[:, v % 2, g * P:(g + 1) * P], vblk[:, g, :],
                                             start=True, stop=True)
                        last.then_inc(pvc_mm, 1)
                pe.wait_ge(mask_r, 2)
                pe.wait_ge(pc_done, CH)
                for p in range(len(PAIRS) + 2):
                    if p < len(PAIRS):
                        c, br, hp = PAIRS[p]
                        bank = pair_bank(p)
                        wait(pe, exp_done, 2 * p - 2)
                        for hd in (2 * hp, 2 * hp + 1):
                            pe.matmul(bank[:, hd % 2, 0:(c + 1) * P], nq[side_of(hd), hp, c * P:(c + 1) * P],
                                      kd[side_of(hd), br, hd // 4, 0:(c + 1) * P], start=True, stop=False)
                        for hd in range(2):
                            last = pe.matmul(bank[:, hd, c * P:(c + 1) * P], ident_r[:, :], causal_r[:, :], start=False, stop=True)
                        last.then_inc(s_mm, 1)
                    v = p - 1
                    if 0 <= v < len(PAIRS):
                        c = PAIRS[v][0]
                        pe.wait_ge(exp_done, 2 * v + 2)
                        wait(pe, pt_done, v)
                        for hd in range(2):
                            for kb in range(c + 1):
                                last = pe.transpose(tr[:, hd, kb * P:(kb + 1) * P], ex[:, 2 * (v % 2) + hd, kb * P:(kb + 1) * P], ident[:, :])
                        last.then_inc(t_mm, 1)
                    v = p - 2
                    if v >= 0:
                        c, br, hp = PAIRS[v]
                        pe.wait_ge(pt_done, v + 1)
                        if hp == 0:
                            pe.wait_ge(ocmp_done, CH)
                            wait(pe, o_rd, 2 * c + br)
                        for hd in (2 * hp, 2 * hp + 1):
                            for kb in range(c + 1):
                                last = pe.matmul(acc[:, 2 + hd // 8, (hd % 8) * HD:(hd % 8 + 1) * HD], pt[:, 2 * (v % 2) + hd % 2, kb * P:(kb + 1) * P],
                                                 vt[:, br, kb, (hd // 4) * HD:(hd // 4 + 1) * HD], start=kb == 0, stop=kb == c)
                        last.then_inc(pv_mm, 1)
                pe.wait_ge(o_add, 2 * CH)
                pe.wait_ge(o_rd, 2 * CH)
                for t in range(DT):
                    if t >= 2:
                        pe.wait_ge(o_lo_done, t - 1)
                    for c in range(CH):
                        last = pe.transpose(tr[:, t % 2, c * P:(c + 1) * P], otok[:, c, t * P:(t + 1) * P], ident[:, :])
                    last.then_inc(ot_tr, 1)
                    if t >= 2:
                        for j in range(2):
                            piece(L["n_out"], L["o_out"], 1, j, t - 2, o_hi, o_lo)
                for t in range(DT - 2, DT):
                    pe.wait_ge(o_lo_done, t + 1)
                    for j in range(2):
                        piece(L["n_out"], L["o_out"], 1, j, t, o_hi, o_lo)

            def retention(L):
                n0, o0 = L["n_in"], L["o_in"]

                def norm_mean(hd):
                    pe.wait_ge(o_sum, hd * 3)
                    pe.wait_ge(r_ready, 2 * L["b_in"] + 1)
                    pe.matmul(st[:, 0, :], ones[:, :], SS[:, :], start=True, stop=True).then_inc(r_mean_mm, 1)

                def norm_var(hd):
                    pe.wait_ge(ro_csum, hd * 3)
                    pe.matmul(st[:, 0, :], ones[:, :], SS[:, :], start=True, stop=True).then_inc(r_var_mm, 1)

                def head(i):
                    later = not (isinstance(i, int) and i == 0)
                    for j in range(12):
                        slot, bank = (n0 + j) % SLOTS, (o0 + j) % BANKS
                        if not later and j == 0:
                            entry_unit(L["b_in"], n0, slot, bank)
                            continue
                        pe.wait_ge(lo_done, i * 12 + (n0 + j + 1))
                        wait(pe, acc_free, i * 20 + (o0 + j - BANKS + 1))
                        for k in range(DT):
                            last = product(acc[:, bank, :], w_hi[:, slot, k, :], w_lo[:, slot, k, :],
                                           a_hi[:, k, :], a_lo[:, k, :], k == 0, k == DT - 1)
                        last.then_inc(unit_done, 1)
                        if 5 <= j <= 8:
                            e = j - 5
                            pe.wait_ge(acc_free, i * 20 + (o0 + 4 + e + 1))
                            wait(pe, rv_done, i * 4 + (e - 1))
                            for c in range(CH):
                                last = pe.transpose(tr[:, e % 2, c * P:(c + 1) * P], work[:, 4 + e % 2, c * P:(c + 1) * P], ident[:, :])
                            last.then_inc(rv_tr, 1)
                        if later and j == 1:
                            norm_mean(i)
                        if later and j == 6:
                            norm_var(i)
                    pe.wait_ge(rope_out, i * 2 + 2)
                    for m in range(CH):
                        bank = (o0 + m) % BANKS
                        pe.wait_ge(acc_free, i * 20 + (o0 + 12 + m - BANKS + 1))
                        for k in range(2):
                            last = pe.matmul(acc[:, bank, 0:SEQ - m * P], rk[:, k, m * P:(m + 1) * P], rq[:, k, m * P:SEQ],
                                             start=k == 0, stop=k == 1)
                        last.then_inc(rs_done, 1)
                    pe.wait_ge(rv_done, i * 4 + 4)
                    for e in range(4):
                        bank = (o0 + e) % BANKS
                        pe.wait_ge(acc_free, i * 20 + (o0 + 16))
                        for m in range(CH):
                            last = pe.matmul(acc[:, bank, m * P:SEQ], rv[:, m, e * P:(e + 1) * P], rp[m][:, :],
                                             start=m == 0, stop=m == CH - 1)
                        last.then_inc(ro_done, 1)
                loop(pe, RH, head, 1)
                norm_mean(RH)

                def last_var(i, j):
                    if isinstance(i, int) and i == 0 and j == 0:
                        norm_var(RH)
                dense(L["n_out"], L["o_out"], 2, 8, TWO, y_hi, y_lo, after=last_var, operand=(y_lo_done, 0))

            pe.wait_ge(params, 16)
            pe.wait_ge(ones_ready, 1)
            pe.wait_ge(id_in, 16)
            pe.wait_ge(params, 16)
            pe.transpose(tr[:, 0, 0:P], rows[:, :], ident[:, :]).then_inc(cols_done, 1)
            pe.wait_ge(params, 80)
            pe.transpose(tr[:, 1, 0:112], rows[0:112, :], ident[0:112, 0:112]).then_inc(cols_done, 1)
            pe.wait_ge(x_in, 16 * CH)
            pe.wait_ge(gain_ready, 2)
            for t in range(DT):
                wait(pe, h_init, t - 1)
                for c in range(CH):
                    last = pe.transpose(tr[:, t % 2, c * P:(c + 1) * P], x_tok[:, c, t * P:(t + 1) * P], ident[:, :])
                last.then_inc(x_tr, 1)
            for L in PL:
                z = L["z"]
                if L["kind"] == 0:
                    dense(L["n_in"], L["o_in"], 4, 4, ONE, a_hi, a_lo, entry=L["b_in"])

                    def mean(i, j, z=z):
                        if isinstance(i, int) and j == 1:
                            pe.wait_ge(vsum, 17 * (z + 1))
                            pe.wait_ge(r_ready, 2 * L["b_in"] + 1)
                            pe.matmul(st[:, 0, :], ones[:, :], SS[:, :], start=True, stop=True).then_inc(mean_mm, 1)
                    dense(L["n_in"] + 16, L["o_in"] + 16, 4, 4, ONE, a_hi, a_lo, 1, mean)
                    gmlp_mix(L)
                    dense(L["n_out"], L["o_out"], 2, 8, TWO, g_hi, g_lo, begun=3)
                if L["kind"] == 1:
                    attention(L)
                    dense(L["n_out"], L["o_out"], 2, 4, ONE, o_hi, o_lo, begun=2)
                if L["kind"] == 2:
                    retention(L)
                boundary(L["b_mid"])
                dense(L["n_up"], L["o_up"], 11, 4, ONE, a_hi, a_lo, entry=L["b_mid"])
                dense(L["n_down"], L["o_down"], 2, 12, THREE, hid_hi, hid_lo, operand=(hid_lo_done, L["q_up"]))
                boundary(L["b_end"])
            pe.wait_ge(h_new, DT * N_BOUND)
            for c in range(CH):
                for half in range(2):
                    k = 2 * c + half
                    wait(pe, y_sb, k - 1)
                    for t in range(4):
                        last = pe.transpose(tr[:, half, t * P:(t + 1) * P], h[:, half * 4 + t, c * P:(c + 1) * P], ident[:, :])
                    last.then_inc(y_tr, 1)

        @block.scalar
        def _(act):
            def split_hi(n, slot):
                if isinstance(n, int) and n >= N_UNITS:
                    return
                act.wait_ge(loaded[slot], n_to_load(n, slot))
                wait(act, unit_done, n - SLOTS + 1)
                act.activation(w_hi[:, slot, :, :], w_raw[:, slot, :, :], ACT.Copy).then_inc(hi_done, 1)

            def n_to_load(n, slot):
                return load_count[0]

            load_count = [None]

            def ahead(n0, i, U, j):
                m = n0 + j + AHEAD
                load_count[0] = i * (16 * U // SLOTS) + 16 * (m // SLOTS + 1)
                split_hi(i * U + m, m % SLOTS)

            def residual(L_n, o0, b, iters, U, G, peel_last=0):
                def step(i):
                    for j in range(U):
                        ahead(L_n, i, U, j)
                        if j % G == G - 1:
                            t = j // G
                            act.wait_ge(acc_free, i * (U // G) + (o0 + t + 1))
                            wait(act, ss_sum, i * (U // G) + (9 * (b - 1) + t))
                            act.activation(sq[:, t % 2, :], F[:, i * (U // G) + t, :], ACT.Square).then_inc(f_sq, 1)
                loop(act, iters, step, 1 if b == 1 else 0, peel_last)

            def boundary(b, last=False):
                if b:
                    act.activation(r4[:, 7:8], ones[:, 0:1], ACT.Sqrt)
                    act.wait_ge(stat_rd, 2 * b)
                    act.activation(r4[:, 0:CH], r4[:, 0:CH], ACT.Sqrt).then_inc(root_done, 1)
                if last:
                    return
                for t in range(DT):
                    if b:
                        act.wait_ge(h_new, DT * (b - 1) + t + 1)
                    else:
                        act.wait_ge(h_init, t + 1)
                    act.activation(a_hi[:, t, :], h[:, t, :], ACT.Copy, scale=gain[:, gain_of(b), t:t + 1]).then_inc(a_hi_done, 1)
                    if t >= 2:
                        wait(act, stat_h, DT * b + t - 1)
                    elif b:
                        wait(act, stat_f, b)
                    act.activation(sq[:, t % 2, :], h[:, t, :], ACT.Square).then_inc(h_sq, 1)
                act.wait_ge(stat_rd, 2 * b + 1)
                act.activation(R[:, :], R[:, :], ACT.Sqrt).then_inc(root_done, 1)

            def gain_of(b):
                return 4 * PL[b // 2]["layer"] + 2 * (b % 2)

            def duplicate(v):
                kind = NSA_UNITS[v][1]
                i, t = nth(v, ROPED), nth(v, (kind,))
                br = 0 if kind == "ks" else 1
                act.wait_ge(n_rope, i + 1)
                for side in range(2):
                    for to in range(2):
                        last = act.activation(kd[to * HD:(to + 1) * HD, br, 2 * t + side, :], work[side * HD:(side + 1) * HD, 2 + v % 2, :], ACT.Copy)
                last.then_inc(kd_dup, 1)

            act.wait_ge(gain_ready, 2)
            for n in range(AHEAD):
                load_count[0] = 16
                split_hi(n, n)
            boundary(0)
            for L in PL:
                z, b = L["z"], L["b_in"]
                if L["kind"] == 0:
                    def gelu_v(i):
                        for j in range(4):
                            ahead(L["n_in"], i, 4, j)
                            act.wait_ge(acc_free, i * 4 + (L["o_in"] + j + 1))
                            m = i * 4 + j
                            act.activation(gv[:, m, :], gv[:, m, :], ACT.Gelu_apprx_tanh).then_inc(gelu_done, 1)
                    loop(act, 4, gelu_v, 1 if L["n_in"] == 0 else 0)

                    def square(m, slot):
                        act.wait_ge(v_cen, m + (GM_TILES * z + 1))
                        act.wait_ge(csum, m + 17 * z)
                        act.activation(sq[:, slot, :], gv[:, m, :], ACT.Square).then_inc(c_sq, 1)

                    def gelu_u(i):
                        for j in range(4):
                            ahead(L["n_in"] + 16, i, 4, j)
                            act.wait_ge(acc_free, i * 4 + (L["o_in"] + 16 + j + 1))
                            m = i * 4 + j
                            act.activation(gu[:, m, :], gu[:, m, :], ACT.Gelu_apprx_tanh).then_inc(gelu_done, 1)
                            if isinstance(i, int):
                                if j == 3:
                                    for k in range(4):
                                        square(k, k % 2)
                            else:
                                square(m, j % 2)
                    loop(act, 4, gelu_u, 1)
                    act.activation(r4[:, 7:8], ones[:, 0:1], ACT.Sqrt)
                    act.wait_ge(var_rd, z + 1)
                    act.activation(work[:, 5, :], work[:, 5, :], ACT.Sqrt).then_inc(var_root, 1)
                    act.wait_ge(ws_tr, z + 1)
                    act.activation(ws_hi[:, :, :], tr[:, :, :], ACT.Copy).then_inc(ws_hi_done, 1)
                    M = GM_TILES
                    for k in range(M + 3):
                        if k < M:
                            act.wait_ge(vn_done, M * z + k + 1)
                            wait(act, vt_done, M * z + k - 1)
                            act.activation(work[:, k % 2, :], gv[:, k, :], ACT.Identity,
                                           bias=lnp[:, 32 + M * z + k:33 + M * z + k]).then_inc(vb_done, 1)
                        m = k - 1
                        if 0 <= m < M:
                            act.wait_ge(vt_done, M * z + m + 1)
                            wait(act, mix_done, M * z + m - 1)
                            act.activation(vt_hi[:, m % 2, :, :], tr[:, m % 2, :], ACT.Copy).then_inc(vt_hi_done, 1)
                        m = k - 3
                        if m >= 0:
                            act.wait_ge(pm_done, M * z + m + 1)
                            act.activation(g_hi[:, m, :], work[:, 2 + m % 3, :], ACT.Copy).then_inc(g_hi_done, 1)
                    residual(L["n_out"], L["o_out"], L["b_mid"], 2, 8, 2)
                if L["kind"] == 1:
                    n0, o0 = L["n_in"], L["o_in"]
                    act.dma_start(pos_i[:, :], positions[0, :].partition_broadcast(P)).then_inc(tab_in, 16)
                    act.dma_start(freq[:, :], c_freq).then_inc(tab_in, 16)
                    act.dma_start(perm[:, :], c_perm).then_inc(n_tab_in, 16)
                    act.dma_start(causal[:, :], c_causal).then_inc(n_tab_in, 16)
                    act.dma_start(cmp_bias[:, :, :], c_cmp_bias).then_inc(n_tab_in, 16)
                    act.dma_start(cmp_keep[:, :, :], c_cmp_keep).then_inc(n_tab_in, 16)
                    for br in range(2):
                        for side in range(2 - br):
                            act.dma_start(w2[:, br, :, side * HD:(side + 1) * HD],
                                          nsa_cmp_w2[z, br].rearrange("(k p) n -> p k n", p=P)).then_inc(n_tab_in, 16)
                    for k in range(2):
                        act.wait_ge(trig_ready, L["trig"] + k + 1)
                        dst = n_sin if k == 0 else n_cos
                        act.activation(dst[:, :], dst[:, :], ACT.Sin).then_inc(sin_done, 1)
                    act.wait_ge(n_tab_in, 16 * 7)
                    act.activation(causal_r[:, :], causal[:, :], ACT.Copy).then_inc(mask_r, 1)
                    act.activation(ident_r[:, :], ident[:, :], ACT.Copy).then_inc(mask_r, 1)
                    for u in range(len(NSA_UNITS) + 1):
                        kind = NSA_UNITS[u][1] if u < len(NSA_UNITS) else ""
                        if kind:
                            ahead(n0, 0, 1, u)
                        if kind in ("kc", "vc"):
                            t = nth(u, ("kc", "vc"))
                            act.wait_ge(acc_free, o0 + u + 1)
                            for side in range(2):
                                for l2 in range(2):
                                    last = act.activation(kc2[l2 * HD:(l2 + 1) * HD, t // 2, 2 * (t % 2) + side, 0:SEQ - l2],
                                                          work[side * HD:(side + 1) * HD, u % 2, l2:SEQ], ACT.Copy)
                            last.then_inc(kc_done, 1)
                        if kind == "gate":
                            act.wait_ge(acc_free, o0 + u + 1)
                            act.activation(work[:, u % 2, :], work[:, u % 2, :], ACT.Sigmoid).then_inc(sig_done, 1)
                        v = u - 1
                        kind = NSA_UNITS[v][1] if v >= 0 else ""
                        if kind in VALUES:
                            i = nth(v, VALUES)
                            act.wait_ge(nv_tr, i + 1)
                            src = tr[:, v % 2, :].rearrange("p (c t) -> p c t", c=CH)
                            dst = gt[:, :, :] if kind == "gate" else vt[:, i // 2, :, (i % 2) * P:(i % 2 + 1) * P]
                            act.activation(dst, src, ACT.Copy).then_inc(nv_done, 1)
                        v = u - 2
                        if v >= 0 and NSA_UNITS[v][1] in ("ks", "kw"):
                            duplicate(v)
                    act.wait_ge(unit_done, n0 + len(NSA_UNITS))
                    for br in range(2):
                        act.dma_start(w1[:, br, :, :], nsa_cmp_w1[z, br].rearrange("(j p) n -> p j n", p=P)).then_inc(w1v_in if br else w1k_in, 16)
                    act.wait_ge(n_zero, 4)
                    for br in range(2):
                        act.wait_ge(cmp_mm, 16 * (br + 1))
                        for hh in range(2):
                            src = acc[:, 2 * br + hh, 0:G_NSA * 32].rearrange("p (g n) -> p g n", g=G_NSA)[:, :, 0:N_CMP]
                            dst = h1k[:, hh, :, 0:N_CMP]
                            if br:
                                dst = h1v[:, hh, :, :].rearrange("p g (r n) -> p g r n", n=32)[:, :, :, 0:N_CMP]
                                src = src.unsqueeze(2).broadcast_to([P, G_NSA, 4, N_CMP])
                            act.activation(dst, src,
                                           ACT.Gelu_apprx_tanh).then_inc(h1_done, 1)
                    act.wait_ge(vcmp_mm, 1)
                    for r in range(4):
                        act.activation(vblk[32 * r:32 * r + 32, :, HD * r:HD * (r + 1)],
                                       st[32 * r:32 * r + 32, 0, 0:G_NSA * HD].rearrange("p (g d) -> p g d", g=G_NSA), ACT.Copy).then_inc(vblk_done, 1)
                    for c in range(CH):
                        act.wait_ge(sm_done, c + 1)
                        rows32 = ex[:, c % 2, :].rearrange("p (h n) -> p h n", h=H_NSA)[:, :, 0:N_CMP]
                        act.activation(rows32, rows32, ACT.Exp).then_inc(pexp, 1)
                        act.wait_ge(pc_tr, c + 1)
                        wait(act, pvc_mm, c - 1)
                        act.activation(pt[:, c % 2, :], tr[:, c % 2, :], ACT.Copy).then_inc(pc_t, 1)
                    for p, (c, br, hp) in enumerate(PAIRS):
                        act.wait_ge(max_done, p + 1)
                        wait(act, t_mm, p - 1)
                        if hp == 0:
                            wait(act, rs_inv, 2 * c + br - 1)
                        for hd in range(2):
                            act.activation(ex[:, 2 * (p % 2) + hd, 0:(c + 1) * P], pair_bank(p)[:, hd, 0:(c + 1) * P], ACT.Exp,
                                           bias=nm[:, p % 4, hd:hd + 1], accum_out=rs[:, br, 2 * hp + hd:2 * hp + hd + 1]).then_inc(exp_done, 1)
                    for t in range(DT):
                        act.wait_ge(ot_tr, t + 1)
                        act.activation(o_hi[:, t, :], tr[:, t % 2, :], ACT.Copy).then_inc(o_hi_done, 1)
                    residual(L["n_out"], L["o_out"], L["b_mid"], 2, 4, 1)
                if L["kind"] == 2:
                    act.dma_start(pos_i[:, :], positions[0, :].partition_broadcast(P)).then_inc(tab_in, 16)
                    act.dma_start(freq[:, :], c_freq).then_inc(tab_in, 16)
                    act.dma_start(decay[:, :, :], c_decay).then_inc(tab_in, 16)
                    for k in range(2):
                        act.wait_ge(trig_ready, L["trig"] + k + 1)
                        dst = r_sin if k == 0 else r_cos
                        act.activation(dst[:, :], dst[:, :], ACT.Sin).then_inc(sin_done, 1)

                    def head(i):
                        later = not (isinstance(i, int) and i == 0)
                        for j in range(12):
                            ahead(L["n_in"], i, 12, j)
                            if later and j == 3:
                                squares(i)
                            if later and j == 7:
                                act.wait_ge(r_var_rd, i)
                                act.activation(r_sd[:, :], r_sd[:, :], ACT.Sqrt).then_inc(r_root, 1)
                            if 5 <= j <= 8:
                                e = j - 5
                                act.wait_ge(rv_tr, i * 4 + (e + 1))
                                act.activation(rv[:, :, e * P:(e + 1) * P], tr[:, e % 2, :].rearrange("p (c t) -> p c t", c=CH),
                                               ACT.Copy).then_inc(rv_done, 1)
                            if j >= 8:
                                act.wait_ge(acc_free, i * 20 + (L["o_in"] + j + 1))
                                act.activation(rg[:, j - 8, :], rg[:, j - 8, :], ACT.Silu).then_inc(rg_done, 1)

                    def squares(hd):
                        for e in range(4):
                            act.wait_ge(ro_cen, (hd - 1) * 4 + (e + 1))
                            act.wait_ge(ro_csum, (hd - 1) * 3 + max(e - 1, 0))
                            act.activation(sq[:, e % 2, :], ro[:, e, :], ACT.Square).then_inc(ro_sq, 1)
                    loop(act, RH, head, 1)

                    def split_y(t0, t1):
                        for t in range(t0, t1):
                            act.activation(y_hi[t], ry[:, t, :], ACT.Copy).then_inc(y_hi_done, 1)
                    act.wait_ge(unit_done, L["n_out"])
                    act.wait_ge(ry_done, 4 * RH - 4)
                    split_y(0, 8)
                    act.wait_ge(rs_done, 4 * RH)
                    split_y(8, 12)
                    squares(RH)
                    act.activation(r4[:, 7:8], ones[:, 0:1], ACT.Sqrt)
                    act.wait_ge(r_var_rd, RH)
                    act.activation(r_sd[:, :], r_sd[:, :], ACT.Sqrt).then_inc(r_root, 1)
                    act.wait_ge(ro_done, 4 * RH)
                    act.wait_ge(ry_done, 4 * RH)
                    split_y(12, 16)
                    residual(L["n_out"], L["o_out"], L["b_mid"], 2, 8, 2)
                boundary(L["b_mid"])

                def swiglu(i):
                    for j in range(4):
                        ahead(L["n_up"], i, 4, j)
                        p, q = j // 2, i * 2 + (L["q_up"] + j // 2)
                        if j % 2 == 0:
                            act.wait_ge(acc_free, i * 4 + (L["o_up"] + j + 1))
                            act.activation(work[:, 2 * p, :], work[:, 2 * p, :], ACT.Silu).then_inc(silu_done, 1)
                        else:
                            act.wait_ge(hid_mul, q + 1)
                            act.activation(hid_hi[:, i * 2 + p, :], work[:, 2 * p, :], ACT.Copy).then_inc(hid_hi_done, 1)
                loop(act, 11, swiglu)
                residual(L["n_down"], L["o_down"], L["b_end"], 2, 12, 3, 1 if L is PL[-1] else 0)
                boundary(L["b_end"], L is PL[-1])

        @block.vector
        def _(dve):
            def split_lo(n, slot):
                if isinstance(n, int) and n >= N_UNITS:
                    return
                dve.wait_ge(hi_done, n + 1)
                dve.tensor_tensor(w_lo[:, slot, :, :], w_raw[:, slot, :, :], w_hi[:, slot, :, :].bitcast(f32),
                                  ALU.subtract).then_inc(lo_done, 1)

            def ahead(n0, i, U, j):
                m = n0 + j + AHEAD
                split_lo(i * U + m, m % SLOTS)

            def leave(n, dst, bank, scale=None):
                dve.wait_ge(unit_done, n + 1)
                if scale is None:
                    dve.tensor_copy(dst, acc[:, bank, :]).then_inc(acc_free, 1)
                else:
                    dve.tensor_tensor(dst, acc[:, bank, :], scale, ALU.mult).then_inc(acc_free, 1)

            def residual(n0, o0, iters, U, G, peel_last=0):
                def step(i):
                    for j in range(U):
                        ahead(n0, i, U, j)
                        if j % G == G - 1:
                            t = j // G
                            leave(i * U + (n0 + j), F[:, i * (U // G) + t, :], (o0 + t) % BANKS)
                loop(dve, iters, step, 0, peel_last)

            def boundary(b, last=False):
                if b:
                    l = PL[(b - 1) // 2]["layer"]
                    g = 4 * l + 2 * ((b - 1) % 2) + 1
                    dve.wait_ge(stat_f, b)
                    dve.tensor_scalar(r4[:, 0:CH], st[:, 0, 0:CH], 1.0 / D_MODEL, RMS_EPS, ALU.mult, ALU.add).then_inc(stat_rd, 1)
                    dve.wait_ge(root_done, 2 * b)
                    dve.reciprocal(r4[:, 0:CH], r4[:, 0:CH]).then_inc(r4_ready, 1)
                    dve.wait_ge(r_spread, b)
                    dve.tensor_copy(R[:, :], st[:, 1, :]).then_inc(r_ready, 1)
                    dve.wait_ge(r_ready, 2 * b)
                    for t in range(DT):
                        if t >= 2:
                            wait(dve, h_new, DT * (b - 1) + t - 1)
                        dve.scalar_tensor_tensor(work[:, 4 + t % 2, :], F[:, t, :], gain[:, g, t:t + 1], R[:, :],
                                                 ALU.mult, ALU.mult).then_inc(f_scaled, 1)
                        if t >= 1 and not last:
                            low(b, t - 1)
                    if not last:
                        low(b, DT - 1)
                else:
                    for t in range(DT):
                        dve.wait_ge(x_tr, t + 1)
                        dve.tensor_copy(h[:, t, :], tr[:, t % 2, :]).then_inc(h_init, 1)
                    for t in range(DT):
                        low(b, t)
                if last:
                    return
                dve.wait_ge(stat_h, DT * (b + 1))
                dve.tensor_scalar(R[:, :], st[:, 0, :], 1.0 / D_MODEL, RMS_EPS, ALU.mult, ALU.add).then_inc(stat_rd, 1)
                dve.wait_ge(root_done, 2 * b + 1)
                dve.reciprocal(R[:, :], R[:, :]).then_inc(r_ready, 1)
                dve.wait_ge(r_ready, 2 * b + 1)

            def low(b, t):
                g = 4 * PL[b // 2]["layer"] + 2 * (b % 2)
                dve.wait_ge(a_hi_done, DT * b + t + 1)
                dve.scalar_tensor_tensor(a_lo[:, t, :], h[:, t, :], gain[:, g, t:t + 1], a_hi[:, t, :].bitcast(f32),
                                         ALU.mult, ALU.subtract).then_inc(a_lo_done, 1)

            trig_count = [0]

            def trig(dst_sin, dst_cos, col, tmp):
                def link(ins):
                    trig_count[0] += 1
                    ins.then_inc(trig_step, 1)
                    dve.wait_ge(trig_step, trig_count[0])
                ang, turns = work[:, tmp, :], work[:, tmp + 1, :]
                link(dve.tensor_copy(turns, pos_i[:, :]))
                link(dve.tensor_scalar(ang, turns, freq[:, col:col + 1], None, ALU.mult))
                link(dve.tensor_scalar(turns, ang, 1.0 / (2 * np.pi), ROUNDER, ALU.mult, ALU.add))
                link(dve.tensor_scalar(turns, turns, ROUNDER, None, ALU.subtract))
                for part in TWO_PI:
                    link(dve.scalar_tensor_tensor(ang, turns, -part, ang, ALU.mult, ALU.add))
                link(dve.tensor_scalar(ang, ang, PI, -PI, ALU.min, ALU.max))
                link(dve.tensor_scalar(turns, ang, -1.0, None, ALU.mult))
                link(dve.tensor_tensor(turns, turns, ang, ALU.min))
                dve.tensor_copy(dst_sin, ang).then_inc(trig_ready, 1)
                dve.tensor_scalar(dst_cos, turns, float(np.float32(np.pi / 2)), None, ALU.add).then_inc(trig_ready, 1)

            def attention(L):
                n0, o0 = L["n_in"], L["o_in"]
                step_count = [0]

                def link(ins):
                    step_count[0] += 1
                    ins.then_inc(dve_step, 1)
                    dve.wait_ge(dve_step, step_count[0])

                dve.wait_ge(tab_in, L["tab"] + 32)
                trig(n_sin[:, :], n_cos[:, :], 0, 4)
                dve.wait_ge(sin_done, L["sine"] + 2)
                for u in range(len(NSA_UNITS) + 1):
                    if u < len(NSA_UNITS):
                        kind = NSA_UNITS[u][1]
                        ahead(n0, 0, 1, u)
                        if u >= 2:
                            was = NSA_UNITS[u - 2][1]
                            if was in ROPED:
                                dve.wait_ge(rope_t, nth(u - 2, ROPED) + 1)
                            elif was in VALUES:
                                dve.wait_ge(nv_tr, nth(u - 2, VALUES) + 1)
                            else:
                                dve.wait_ge(kc_done, nth(u - 2, ("kc", "vc")) + 1)
                        dve.wait_ge(unit_done, n0 + u + 1)
                        dst, src = work[:, u % 2, :], acc[:, (o0 + u) % BANKS, :]
                        if kind == "q":
                            dve.scalar_tensor_tensor(dst, src, NSA_SCALE, R[:, :], ALU.mult, ALU.mult).then_inc(acc_free, 1)
                        else:
                            dve.tensor_tensor(dst, src, R[:, :], ALU.mult).then_inc(acc_free, 1)
                    v = u - 1
                    if v >= 0 and NSA_UNITS[v][1] in ROPED:
                        i = nth(v, ROPED)
                        dve.wait_ge(rot_done, i + 1)
                        before = [w for w in range(v) if NSA_UNITS[w][1] in ROPED and w % 2 == v % 2]
                        if before:
                            dve.wait_ge(n_rope, nth(before[-1], ROPED) + 1)
                            if NSA_UNITS[before[-1]][1] != "q":
                                dve.wait_ge(kd_dup, nth(before[-1], ("ks", "kw")) + 1)
                        dve.tensor_tensor(work[:, 2 + v % 2, :], work[:, v % 2, :], n_cos[:, :], ALU.mult)
                        dve.tensor_tensor(work[:, 4 + v % 2, :], tr[:, v % 2, :], n_sin[:, :], ALU.mult).then_inc(rope_t, 1)
                dve.wait_ge(kc_done, 4)
                dve.wait_ge(n_tab_in, 16 * 7)
                for br in range(2):
                    for j in range(16):
                        k = 16 * br + j
                        wait(dve, cmp_mm, k - 1)
                        dve.tensor_scalar(stg[:, j % 2, :, 0:N_CMP], kc2[:, br, :, 2 * j:2 * j + CMP_STRIDE * (N_CMP - 1) + 1:CMP_STRIDE],
                                          lnp[:, 80 + 16 * br + j:81 + 16 * br + j], None, ALU.add).then_inc(stg_ready, 1)
                kx, kt = work[:, 0, 0:G_NSA * N_CMP], work[:, 1, 0:G_NSA * N_CMP]
                kr = work[:, 2, 0:G_NSA * N_CMP]
                ends = slice(CMP_LEN - 1, SEQ, CMP_STRIDE)

                def by_group(ap):
                    return ap.rearrange("p (g n) -> p g n", g=G_NSA)

                def over_groups(table):
                    return table[:, ends].unsqueeze(1).broadcast_to([P, G_NSA, N_CMP])

                dve.wait_ge(kcmp_mm, 1)
                dve.wait_ge(nv_tr, 5)
                dve.wait_ge(n_rope, 12)
                dve.tensor_copy(kx, tr[:, 0, 0:G_NSA * N_CMP]).then_inc(kcmp_x, 1)
                dve.wait_ge(kcmp_x, 1)
                dve.tensor_tensor(by_group(kt), by_group(kx), over_groups(n_cos), ALU.mult)
                dve.wait_ge(kcmp_rot, 1)
                link(dve.tensor_tensor(by_group(kr), by_group(tr[:, 1, 0:G_NSA * N_CMP]), over_groups(n_sin), ALU.mult))
                dve.tensor_tensor(kcr[:, :, 0:N_CMP], by_group(kt), by_group(kr), ALU.add).then_inc(kcmp_done, 1)

                def per_head(ap):
                    return ap.unsqueeze(2).broadcast_to([P, H_NSA, N_CMP])

                def gate(c, branch):
                    return gt[:, c, NSA_GATE0 + branch:NSA_GATE0 + branch + 3 * (H_NSA - 1) + 1:3]

                def compressed_out(c):
                    dve.wait_ge(pvc_mm, c + 1)
                    dve.tensor_tensor(otok[:, c, :].rearrange("p (h d) -> p h d", d=HD), acc[:, 2:4, :].rearrange("p a (h d) -> p (a h) d", d=HD),
                                      csm[:, c, :].unsqueeze(2).broadcast_to([P, H_NSA, HD]), ALU.mult).then_inc(ocmp_done, 1)

                dve.wait_ge(n_zero, 4)
                dve.wait_ge(nv_done, 5)
                for c in range(CH):
                    rows32 = ex[:, c % 2, :].rearrange("p (h n) -> p h n", h=H_NSA)[:, :, 0:N_CMP]
                    scores = acc[:, c % 2, :].rearrange("p (h n) -> p h n", h=H_NSA)[:, :, 0:N_CMP]
                    over = [P, H_NSA, N_CMP]
                    dve.wait_ge(sc_mm, c + 1)
                    wait(dve, pc_tr, c - 1)
                    link(dve.tensor_tensor(rows32, scores, cmp_bias[:, c, 0:N_CMP].unsqueeze(1).broadcast_to(over), ALU.add))
                    link(dve.tensor_reduce(cmx[:, c, :], rows32, AX.X, ALU.max))
                    dve.tensor_tensor(rows32, rows32, per_head(cmx[:, c, :]), ALU.subtract).then_inc(sm_done, 1)
                    dve.wait_ge(pexp, c + 1)
                    link(dve.tensor_tensor(rows32, rows32, cmp_keep[:, c, 0:N_CMP].unsqueeze(1).broadcast_to(over), ALU.mult))
                    link(dve.tensor_reduce(csm[:, c, :], rows32, AX.X, ALU.add))
                    link(dve.tensor_scalar(csm[:, c, :], csm[:, c, :], 1e-30, None, ALU.max))
                    link(dve.reciprocal(csm[:, c, :], csm[:, c, :]))
                    dve.tensor_tensor(csm[:, c, :], csm[:, c, :], gate(c, 0), ALU.mult).then_inc(pc_done, 1)
                    if c >= 1:
                        compressed_out(c - 1)
                dve.wait_ge(pc_done, CH)
                compressed_out(CH - 1)
                n = len(PAIRS)
                for p in range(n + 2):
                    if p < n:
                        c = PAIRS[p][0]
                        dve.wait_ge(s_mm, p + 1)
                        wait(dve, exp_done, 2 * p - 6)
                        dve.tensor_reduce(nm[:, p % 4, :], pair_bank(p)[:, :, 0:(c + 1) * P], AX.X, ALU.max, negate=True).then_inc(max_done, 1)
                    v = p - 1
                    if 0 <= v < n:
                        c = PAIRS[v][0]
                        dve.wait_ge(t_mm, v + 1)
                        wait(dve, pv_mm, v - 1)
                        dve.tensor_copy(pt[:, 2 * (v % 2):2 * (v % 2) + 2, 0:(c + 1) * P], tr[:, :, 0:(c + 1) * P]).then_inc(pt_done, 1)
                    v = p - 2
                    if v >= 0 and PAIRS[v][2] == H_NSA // 2 - 1:
                        c, br, _ = PAIRS[v]
                        grp = 2 * c + br
                        wait(dve, o_rd, grp - 1)
                        link(dve.reciprocal(scl[:, br, :], rs[:, br, :]))
                        dve.tensor_tensor(scl[:, br, :], scl[:, br, :], gate(c, 1 + br), ALU.mult).then_inc(rs_inv, 1)
                        dve.wait_ge(rs_inv, grp + 1)
                        dve.wait_ge(pv_mm, v + 1)
                        wait(dve, o_add, grp - 1)
                        dve.tensor_tensor(work[:, 2 * br:2 * br + 2, :].rearrange("p a (h d) -> p (a h) d", d=HD),
                                          acc[:, 2:4, :].rearrange("p a (h d) -> p (a h) d", d=HD),
                                          scl[:, br, :].unsqueeze(2).broadcast_to([P, H_NSA, HD]), ALU.mult).then_inc(o_rd, 1)
                for t in range(DT):
                    dve.wait_ge(o_hi_done, t + 1)
                    dve.tensor_tensor(o_lo[:, t, :], tr[:, t % 2, :], o_hi[:, t, :].bitcast(f32), ALU.subtract).then_inc(o_lo_done, 1)
                residual(L["n_out"], L["o_out"], 2, 4, 1)

            dve.memset(ones[:, :], 1.0).then_inc(ones_ready, 1)
            dve.wait_ge(cols_done, 1)
            dve.tensor_copy(gain[:, :, :], tr[:, 0, 0:P]).then_inc(gain_ready, 1)
            dve.wait_ge(cols_done, 2)
            dve.tensor_copy(lnp[:, :], tr[:, 1, 0:112]).then_inc(gain_ready, 1)
            dve.wait_ge(gain_ready, 2)
            for n in range(AHEAD):
                split_lo(n, n)
            boundary(0)
            for L in PL:
                z, b = L["z"], L["b_in"]
                if L["kind"] == 0:
                    n0, o0, M = L["n_in"], L["o_in"], GM_TILES

                    def values(i):
                        for j in range(4):
                            ahead(n0, i, 4, j)
                            leave(i * 4 + (n0 + j), gv[:, i * 4 + j, :], (o0 + j) % BANKS, R[:, :])
                    loop(dve, 4, values)

                    def centre(m):
                        dve.tensor_tensor(gv[:, m, :], gv[:, m, :], work[:, 4, :], ALU.subtract).then_inc(v_cen, 1)

                    def gates(i):
                        for j in range(4):
                            ahead(n0 + 16, i, 4, j)
                            leave(i * 4 + (n0 + 16 + j), gu[:, i * 4 + j, :], (o0 + 16 + j) % BANKS, R[:, :])
                            if not isinstance(i, int):
                                centre(i * 4 + j)
                            elif j == 2:
                                dve.wait_ge(mean_mm, z + 1)
                                dve.tensor_scalar(work[:, 4, :], st[:, 0, :], 1.0 / GM_WIDTH, None, ALU.mult).then_inc(mu_ready, 1)
                            elif j == 3:
                                dve.wait_ge(mu_ready, z + 1)
                                for k in range(4):
                                    centre(k)
                    loop(dve, 4, gates, 1)
                    dve.wait_ge(var_mm, z + 1)
                    dve.tensor_scalar(work[:, 5, :], st[:, 0, :], 1.0 / GM_WIDTH, LN_EPS, ALU.mult, ALU.add).then_inc(var_rd, 1)
                    dve.wait_ge(ws_hi_done, z + 1)
                    dve.tensor_tensor(ws_lo[:, :, :].rearrange("p (a g) t -> p a (g t)", a=2), tr[:, :, :],
                                      ws_hi[:, :, :].rearrange("p (a g) t -> p a (g t)", a=2).bitcast(f32),
                                      ALU.subtract).then_inc(ws_lo_done, 1)
                    dve.wait_ge(var_root, z + 1)
                    dve.reciprocal(work[:, 5, :], work[:, 5, :]).then_inc(rstd_ready, 1)
                    dve.wait_ge(rstd_ready, z + 1)
                    dve.wait_ge(bs_in, 16 * (z + 1))
                    for k in range(-2, M + 2):
                        v = k + 2
                        if v < M:
                            dve.scalar_tensor_tensor(gv[:, v, :], gv[:, v, :], lnp[:, M * z + v:M * z + v + 1], work[:, 5, :],
                                                     ALU.mult, ALU.mult).then_inc(vn_done, 1)
                        m = k - 1
                        if 0 <= m < M:
                            dve.wait_ge(vt_hi_done, M * z + m + 1)
                            dve.tensor_tensor(vt_lo[:, m % 2, :, :].rearrange("p c t -> p (c t)"), tr[:, m % 2, :],
                                              vt_hi[:, m % 2, :, :].rearrange("p c t -> p (c t)").bitcast(f32),
                                              ALU.subtract).then_inc(vt_lo_done, 1)
                        m = k - 2
                        if m >= 0:
                            dve.wait_ge(mix_done, M * z + m + 1)
                            if m >= 3:
                                dve.wait_ge(g_lo_done, M * z + m - 2)
                            dve.tensor_tensor(work[:, 2 + m % 3, :].rearrange("p (c t) -> p c t", c=CH),
                                              acc[:, mix_bank(L, m), :].rearrange("p (c t) -> p c t", c=CH),
                                              bs[:, m // 2, :].unsqueeze(1).broadcast_to([P, CH, P]),
                                              ALU.add).then_inc(xb_done, 1)
                    residual(L["n_out"], L["o_out"], 2, 8, 2)
                if L["kind"] == 1:
                    attention(L)
                if L["kind"] == 2:
                    n0, o0 = L["n_in"], L["o_in"]
                    dve.wait_ge(tab_in, L["tab"] + 48)
                    trig(r_sin[:, :], r_cos[:, :], 1, 0)
                    dve.wait_ge(sin_done, L["sine"] + 2)
                    dve.tensor_tensor(r_sin[:, :], r_sin[:, :], R[:, :], ALU.mult).then_inc(trig_ready, 1)
                    dve.tensor_tensor(r_cos[:, :], r_cos[:, :], R[:, :], ALU.mult).then_inc(trig_ready, 1)
                    dve.wait_ge(trig_ready, L["trig"] + 4)

                    def rotate(i, j, k):
                        dve.wait_ge(unit_done, i * 12 + (n0 + j + 1))
                        wait(dve, rope_out, i * 2 + k)
                        A, Bk = acc[:, (o0 + j - 1) % BANKS, :], acc[:, (o0 + j) % BANKS, :]
                        dve.tensor_tensor(work[:, 0, :], A, r_cos[:, :], ALU.mult)
                        dve.tensor_tensor(work[:, 1, :], A, r_sin[:, :], ALU.mult).then_inc(acc_free, 1)
                        dve.tensor_tensor(work[:, 2, :], Bk, r_sin[:, :], ALU.mult)
                        dve.tensor_tensor(work[:, 3, :], Bk, r_cos[:, :], ALU.mult).then_inc(acc_free, 1)

                    def centre(hd):
                        dve.wait_ge(r_mean_mm, hd)
                        dve.tensor_scalar(r_mu[:, :], st[:, 0, :], 1.0 / R_V, None, ALU.mult).then_inc(r_mu_ready, 1)
                        dve.wait_ge(r_mu_ready, hd)
                        for e in range(4):
                            dve.tensor_tensor(ro[:, e, :], ro[:, e, :], r_mu[:, :], ALU.subtract).then_inc(ro_cen, 1)

                    def variance(hd):
                        dve.wait_ge(r_var_mm, hd)
                        dve.tensor_scalar(r_sd[:, :], st[:, 0, :], 1.0 / R_V, LN_EPS, ALU.mult, ALU.add).then_inc(r_var_rd, 1)

                    def finish_head(hd):
                        dve.wait_ge(r_root, hd)
                        dve.reciprocal(r_sd[:, :], r_sd[:, :]).then_inc(r_sd_ready, 1)
                        dve.wait_ge(r_sd_ready, hd * 5 - 4)
                        dve.wait_ge(rg_done, hd * 4)
                        for e in range(4):
                            dve.tensor_tensor(ro[:, e, :], ro[:, e, :], r_sd[:, :], ALU.mult).then_inc(r_sd_ready, 1)
                        for e in range(4):
                            dve.wait_ge(r_sd_ready, hd * 5 + (e - 3))
                            t = (hd - 1) * 4 + e
                            dve.scalar_tensor_tensor(ry[:, t, :], ro[:, e, :],
                                                     lnp[:, bass.ds(t + 64, 1)] if not isinstance(t, int) else lnp[:, 64 + t:65 + t],
                                                     rg[:, e, :], ALU.mult, ALU.mult).then_inc(ry_done, 1)

                    def head(i):
                        later = not (isinstance(i, int) and i == 0)
                        for j in range(12):
                            ahead(n0, i, 12, j)
                            if j == 1:
                                rotate(i, 1, 0)
                            elif j == 3:
                                rotate(i, 3, 1)
                            elif 4 <= j < 8:
                                e = j - 4
                                wait(dve, rv_tr, i * 4 + (e - 1))
                                dve.wait_ge(unit_done, i * 12 + (n0 + j + 1))
                                dve.tensor_tensor(work[:, 4 + e % 2, :], acc[:, (o0 + j) % BANKS, :], R[:, :], ALU.mult).then_inc(acc_free, 1)
                            elif j >= 8:
                                if later and j == 8:
                                    dve.wait_ge(ry_done, i * 4)
                                leave(i * 12 + (n0 + j), rg[:, j - 8, :], (o0 + j) % BANKS, R[:, :])
                            if later:
                                if j == 2:
                                    centre(i)
                                if j == 7:
                                    variance(i)
                                    finish_head(i)
                        for m in range(CH):
                            dve.wait_ge(rs_done, i * 4 + (m + 1))
                            dve.scalar_tensor_tensor(rp[m][:, :], acc[:, (o0 + m) % BANKS, 0:SEQ - m * P], R_QK ** -0.5,
                                                     decay[:, i, 0:SEQ - m * P], ALU.mult, ALU.mult).then_inc(acc_free, 1)
                        for e in range(4):
                            dve.wait_ge(ro_done, i * 4 + (e + 1))
                            dve.tensor_copy(ro[:, e, :], acc[:, (o0 + e) % BANKS, :]).then_inc(acc_free, 1)
                    loop(dve, RH, head, 1)

                    def split_y(t0, t1):
                        for t in range(t0, t1):
                            dve.wait_ge(y_hi_done, t + 1)
                            dve.tensor_tensor(y_lo[:, t, :], ry[:, t, :], y_hi[t].bitcast(f32), ALU.subtract).then_inc(y_lo_done, 1)
                    centre(RH)
                    split_y(0, 8)
                    variance(RH)
                    split_y(8, 12)
                    finish_head(RH)
                    split_y(12, 16)
                    residual(L["n_out"], L["o_out"], 2, 8, 2)
                boundary(L["b_mid"])

                def swiglu(i):
                    for j in range(4):
                        ahead(L["n_up"], i, 4, j)
                        if j % 2 == 0:
                            wait(dve, hid_lo_done, i * 2 + (L["q_up"] + j // 2 - 1))
                        leave(i * 4 + (L["n_up"] + j), work[:, j, :], (L["o_up"] + j) % BANKS, R[:, :])
                loop(dve, 11, swiglu, 1 if L["q_up"] == 0 else 0)
                residual(L["n_down"], L["o_down"], 2, 12, 3, 1 if L is PL[-1] else 0)
                boundary(L["b_end"], L is PL[-1])
            for k in range(2 * CH):
                dve.wait_ge(y_tr, k + 1)
                dve.tensor_copy(y_tok[:, k // 2, (k % 2) * SEQ:(k % 2 + 1) * SEQ], tr[:, k % 2, :]).then_inc(y_sb, 1)

        @block.gpsimd
        def _(pool):
            def residual_sum(b, iters, T):
                pool.memset(SS[:, :], 0.0).then_inc(ss_sum, 1)

                def step(i):
                    for t in range(T):
                        k = i * T + t
                        pool.wait_ge(f_sq, k + (DT * (b - 1) + 1))
                        pool.wait_ge(ss_sum, k + (9 * (b - 1) + 1))
                        pool.tensor_tensor(SS[:, :], SS[:, :], sq[:, t % 2, :], ALU.add).then_inc(ss_sum, 1)
                loop(pool, iters, step)

            def boundary(b):
                if b:
                    for t in range(DT):
                        pool.wait_ge(f_scaled, DT * (b - 1) + t + 1)
                        pool.tensor_tensor(h[:, t, :], h[:, t, :], work[:, 4 + t % 2, :], ALU.add).then_inc(h_new, 1)

            pool.dma_start(ident[:, :], c_identity).then_inc(id_in, 16)
            for c in range(CH):
                pool.dma_start(x_tok[:, c, :], x[0, c * P:(c + 1) * P, :]).then_inc(x_in, 16)
            boundary(0)
            for L in PL:
                z, b = L["z"], L["b_in"]
                if L["kind"] == 0:
                    M = GM_TILES
                    pool.memset(SS[:, :], 0.0).then_inc(vsum, 1)

                    def add_v(i):
                        for j in range(4):
                            m = i * 4 + j
                            pool.wait_ge(gelu_done, m + (2 * M * z + 1))
                            pool.wait_ge(vsum, m + (17 * z + 1))
                            pool.tensor_tensor(SS[:, :], SS[:, :], gv[:, m, :], ALU.add).then_inc(vsum, 1)
                    loop(pool, 4, add_v)
                    pool.wait_ge(ws_in, 16 * (z + 1))
                    pool.affine_select(out=ws_raw[:, :, :], in_=ws_raw[:, :, :], compare_op=ALU.is_ge, fill=0.0, base=0,
                                       pattern=[[0, GM_GROUPS], [-1, P]], channel_multiplier=1).then_inc(ws_masked, 1)
                    pool.wait_ge(mu_ready, z + 1)
                    pool.memset(SS[:, :], 0.0).then_inc(csum, 1)

                    def add_c(i):
                        for j in range(4):
                            m = i * 4 + j
                            pool.wait_ge(c_sq, m + (M * z + 1))
                            pool.wait_ge(csum, m + (17 * z + 1))
                            pool.tensor_tensor(SS[:, :], SS[:, :], sq[:, j % 2, :], ALU.add).then_inc(csum, 1)
                    loop(pool, 4, add_c)
                    for k in range(M + 1):
                        if k < M:
                            pool.wait_ge(xb_done, M * z + k + 1)
                            pool.tensor_tensor(work[:, 2 + k % 3, :], work[:, 2 + k % 3, :], gu[:, k, :], ALU.mult).then_inc(pm_done, 1)
                        m = k - 1
                        if m >= 0:
                            pool.wait_ge(g_hi_done, M * z + m + 1)
                            pool.tensor_tensor(g_lo[:, m, :], work[:, 2 + m % 3, :], g_hi[:, m, :].bitcast(f32),
                                               ALU.subtract).then_inc(g_lo_done, 1)
                    residual_sum(L["b_mid"], 2, 4)
                if L["kind"] == 1:
                    pool.wait_ge(a_lo_done, DT * (b + 1))
                    pool.memset(h1v[:, :, :, :], 0.0).then_inc(n_zero, 1)
                    pool.memset(vblk[:, :, :], 0.0).then_inc(n_zero, 1)
                    pool.memset(ex[:, 0, :], 0.0).then_inc(n_zero, 1)
                    pool.memset(ex[:, 1, :], 0.0).then_inc(n_zero, 1)
                    for u, (_, kind) in enumerate(NSA_UNITS):
                        if kind not in ROPED:
                            continue
                        pool.wait_ge(rope_t, nth(u, ROPED) + 1)
                        t1, t2 = work[:, 2 + u % 2, :], work[:, 4 + u % 2, :]
                        if kind == "q":
                            pool.tensor_tensor(nq[:, u, :], t1, t2, ALU.add).then_inc(n_rope, 1)
                        else:
                            pool.tensor_tensor(t1, t1, t2, ALU.add).then_inc(n_rope, 1)
                    for grp in range(2 * CH):
                        pool.wait_ge(ocmp_done, CH)
                        pool.wait_ge(o_rd, grp + 1)
                        if grp:
                            pool.wait_ge(o_add, grp)
                        c, br = grp // 2, grp % 2
                        pool.tensor_tensor(otok[:, c, :], otok[:, c, :], work[:, 2 * br:2 * br + 2, :].rearrange("p a t -> p (a t)"), ALU.add).then_inc(o_add, 1)
                    residual_sum(L["b_mid"], 2, 4)
                if L["kind"] == 2:
                    o0 = L["o_in"]

                    def head(i):
                        later = not (isinstance(i, int) and i == 0)
                        for k in range(2):
                            dst = rq if k == 0 else rk
                            pool.wait_ge(acc_free, i * 20 + (o0 + 2 * k + 2))
                            if later:
                                pool.wait_ge(rs_done, i * 4)
                            pool.tensor_tensor(dst[:, 0, :], work[:, 0, :], work[:, 2, :], ALU.subtract)
                            pool.tensor_tensor(dst[:, 1, :], work[:, 3, :], work[:, 1, :], ALU.add).then_inc(rope_out, 1)
                            if later and k == 0:
                                square_sum(i)
                        output_sum(i)

                    def output_sum(i):
                        if not (isinstance(i, int) and i == 0):
                            pool.wait_ge(r_var_rd, i)
                        for e in range(1, 4):
                            pool.wait_ge(acc_free, i * 20 + (o0 + 16 + e + 1))
                            if e > 1:
                                pool.wait_ge(o_sum, i * 3 + (e - 1))
                            pool.tensor_tensor(SS[:, :], ro[:, 0, :] if e == 1 else SS[:, :], ro[:, e, :], ALU.add).then_inc(o_sum, 1)

                    def square_sum(hd):
                        pool.wait_ge(r_mu_ready, hd)
                        for e in range(1, 4):
                            pool.wait_ge(ro_sq, (hd - 1) * 4 + (e + 1))
                            if e > 1:
                                pool.wait_ge(ro_csum, (hd - 1) * 3 + (e - 1))
                            pool.tensor_tensor(SS[:, :], sq[:, 0, :] if e == 1 else SS[:, :], sq[:, e % 2, :], ALU.add).then_inc(ro_csum, 1)
                    loop(pool, RH, head, 1)
                    square_sum(RH)
                    pool.wait_ge(r_var_rd, RH)
                    residual_sum(L["b_mid"], 2, 4)
                boundary(L["b_mid"])

                def swiglu(i):
                    for p in range(2):
                        q = i * 2 + (L["q_up"] + p)
                        pool.wait_ge(silu_done, q + 1)
                        pool.wait_ge(acc_free, i * 4 + (L["o_up"] + 2 * p + 2))
                        pool.tensor_tensor(work[:, 2 * p, :], work[:, 2 * p, :], work[:, 2 * p + 1, :], ALU.mult).then_inc(hid_mul, 1)
                        pool.wait_ge(hid_hi_done, q + 1)
                        pool.tensor_tensor(hid_lo[:, i * 2 + p, :], work[:, 2 * p, :], hid_hi[:, i * 2 + p, :].bitcast(f32),
                                           ALU.subtract).then_inc(hid_lo_done, 1)
                loop(pool, 11, swiglu)
                residual_sum(L["b_end"], 2, 4)
                boundary(L["b_end"])


def constants():
    p = np.arange(P)
    freq = np.stack([ROPE_THETA ** -((p % 32) / 32.0), ROPE_THETA ** -(p / 128.0)], 1)
    log_gamma = np.log1p(-(2.0 ** (-5.0 - np.arange(RH))))
    rel = np.arange(SEQ)[None, :] - p[:, None]
    decay = np.where(rel[:, None, :] >= 0, np.exp(log_gamma[None, :, None] * np.maximum(rel, 0)[:, None, :]), 0.0)
    perm = np.zeros((P, P))
    for base in (0, HD):
        for d in range(HD // 2):
            perm[base + d + HD // 2, base + d] = -1.0
            perm[base + d, base + d + HD // 2] = 1.0
    causal = np.where(p[None, :] <= p[:, None], 0.0, MASKED)
    ends = CMP_STRIDE * np.arange(32) + CMP_LEN - 1
    seen = (ends[None, None, :] <= (p[:, None, None] + P * np.arange(CH)[None, :, None])) & (np.arange(32) < N_CMP)
    nsa = {"c_perm": perm, "c_causal": causal, "c_cmp_bias": np.where(seen, 0.0, MASKED), "c_cmp_keep": np.where(seen, 1.0, 0.0)}
    return {"c_identity": np.eye(P, dtype=np.float32), "c_freq": freq.astype(np.float32), "c_decay": decay.astype(np.float32),
            **{name: a.astype(np.float32) for name, a in nsa.items()}}


_INS = ["x", "positions", "norm_g", "ffn_w_gate", "ffn_w_up", "ffn_w_down", "gm_w_in", "gm_ln_g", "gm_ln_b",
        "gm_w_s", "gm_b_s", "gm_w_out", "nsa_w_in", "nsa_cmp_pe", "nsa_cmp_w1", "nsa_cmp_w2", "nsa_w_out",
        "ret_w_in", "ret_gn_g", "ret_w_out"]


def kernel(**inputs):
    import concourse.bacc as bacc
    from concourse.bass_utils import run_bass_kernel_spmd

    nc = bacc.Bacc("TRN2", target_bir_lowering=False, num_devices=1)
    arrays = {name: np.ascontiguousarray(inputs[name]) for name in _INS}
    arrays.update(constants())
    args = [nc.dram_tensor(name, a.shape, mybir.dt.from_np(a.dtype), kind="ExternalInput").ap() for name, a in arrays.items()]
    args.append(nc.dram_tensor("out", (1, SEQ, D_MODEL), f32, kind="ExternalOutput").ap())
    build(nc, *args)
    r = run_bass_kernel_spmd(nc, [arrays], core_ids=[0])
    return r.results[0]["out"]
```
